# Optimizing a Trainium2 kernel written in Bass

```python
import math
import jax, jax.numpy as jnp
from jax import lax
import numpy as np

D_MODEL = 2048
BATCH = 1
SEQ = 512
DEPTH = 1

HEAD_DIM = 64
DIFF_HEADS = D_MODEL // 4 // (2 * HEAD_DIM)
FOX_HEADS = D_MODEL // 4 // HEAD_DIM
NSA_HEADS = D_MODEL // 2 // HEAD_DIM
NSA_GROUPS = 4
NSA_HPG = NSA_HEADS // NSA_GROUPS
CMP_BLOCK = 32
CMP_STRIDE = 16
CMP_HIDDEN = 256
SEL_BLOCK = 64
SEL_TOPK = 16
WINDOW = 512
QBLK = 128
NUM_BUCKETS = 32
MAX_DISTANCE = 128
N_GROUPS = 8
EXPERTS_PER_GROUP = 8
N_EXPERTS = N_GROUPS * EXPERTS_PER_GROUP
TOP_K_EXPERTS = 2
D_EXPERT = D_MODEL // 8
MOE_CHUNK = 128
RMS_EPS = 1e-6
NEG_INF = -1e30
SEL_FORCE = 1e4

SPLIT_SIZES = (
    DIFF_HEADS * 2 * HEAD_DIM,
    DIFF_HEADS * 2 * HEAD_DIM,
    DIFF_HEADS * 2 * HEAD_DIM,
    FOX_HEADS * HEAD_DIM,
    FOX_HEADS * HEAD_DIM,
    FOX_HEADS * HEAD_DIM,
    FOX_HEADS,
    NSA_HEADS * HEAD_DIM,
    NSA_GROUPS * HEAD_DIM,
    NSA_GROUPS * HEAD_DIM,
    NSA_GROUPS * HEAD_DIM,
    NSA_GROUPS * HEAD_DIM,
    NSA_GROUPS * HEAD_DIM,
    NSA_GROUPS * HEAD_DIM,
    3 * NSA_HEADS,
)
D_IN = sum(SPLIT_SIZES)
D_MIX = DIFF_HEADS * 2 * HEAD_DIM + FOX_HEADS * HEAD_DIM + NSA_HEADS * HEAD_DIM

kernel_name = "hybrid_diff_fox_nsa_hmoe"

def rms_norm(x, g):
    x32 = x.astype(jnp.float32)
    y = x32 * lax.rsqrt(jnp.mean(x32 * x32, axis=-1, keepdims=True) + RMS_EPS)
    return (y * g.astype(jnp.float32)).astype(x.dtype)

def masked_softmax(logits, mask):
    return jax.nn.softmax(jnp.where(mask, logits, NEG_INF), axis=-1)

def t5_bucket(rel):
    n = jnp.maximum(rel, 0)
    max_exact = NUM_BUCKETS // 2
    nf = jnp.maximum(n, max_exact).astype(jnp.float32)
    large = max_exact + (jnp.log(nf / max_exact) / math.log(MAX_DISTANCE / max_exact)
                         * (NUM_BUCKETS - max_exact)).astype(jnp.int32)
    return jnp.where(n < max_exact, n, jnp.minimum(large, NUM_BUCKETS - 1))

def diff_attention(q, k, v, lam, bias_table):
    B, S, H = q.shape[:3]
    scale = HEAD_DIM ** -0.5
    kpos = jnp.arange(S)
    k1, k2 = k[:, :, :, 0], k[:, :, :, 1]
    table = bias_table.astype(jnp.float32)

    def block(i):
        q0 = i * QBLK
        qb = lax.dynamic_slice_in_dim(q, q0, QBLK, axis=1)
        rel = (q0 + jnp.arange(QBLK))[:, None] - kpos[None, :]
        mask = rel >= 0
        bias = jnp.transpose(table[t5_bucket(rel)], (2, 0, 1))
        s1 = jnp.einsum('bqhd,bkhd->bhqk', qb[:, :, :, 0], k1).astype(jnp.float32) * scale + bias
        s2 = jnp.einsum('bqhd,bkhd->bhqk', qb[:, :, :, 1], k2).astype(jnp.float32) * scale + bias
        a = masked_softmax(s1, mask) - lam * masked_softmax(s2, mask)
        return jnp.einsum('bhqk,bkhd->bqhd', a.astype(v.dtype), v)

    out = lax.map(block, jnp.arange(S // QBLK))
    return jnp.moveaxis(out, 0, 1).reshape(B, S, H, v.shape[-1])

def forgetting_attention(q, k, v, f_logit, b_f):
    B, S, H, _ = q.shape
    scale = HEAD_DIM ** -0.5
    kpos = jnp.arange(S)
    log_f = jax.nn.log_sigmoid(f_logit.astype(jnp.float32) + b_f.astype(jnp.float32))
    c = jnp.transpose(jnp.cumsum(log_f, axis=1), (0, 2, 1))

    def block(i):
        q0 = i * QBLK
        qb = lax.dynamic_slice_in_dim(q, q0, QBLK, axis=1)
        cq = lax.dynamic_slice_in_dim(c, q0, QBLK, axis=2)
        mask = (q0 + jnp.arange(QBLK))[:, None] >= kpos[None, :]
        s = (jnp.einsum('bqhd,bkhd->bhqk', qb, k).astype(jnp.float32) * scale
             + cq[..., :, None] - c[..., None, :])
        p = masked_softmax(s, mask)
        return jnp.einsum('bhqk,bkhd->bqhd', p.astype(v.dtype), v)

    out = lax.map(block, jnp.arange(S // QBLK))
    return jnp.moveaxis(out, 0, 1).reshape(B, S, H, HEAD_DIM)

def compress(kv, pos, w1, w2):
    B, S, G, Dh = kv.shape
    n_cmp = (S - CMP_BLOCK) // CMP_STRIDE + 1
    idx = CMP_STRIDE * jnp.arange(n_cmp)[:, None] + jnp.arange(CMP_BLOCK)[None, :]
    blocks = kv[:, idx] + pos[None, None, :, None, :]
    flat = jnp.transpose(blocks, (0, 1, 3, 2, 4)).reshape(B, n_cmp, G, CMP_BLOCK * Dh)
    return jax.nn.gelu(flat @ w1) @ w2

def nsa_attention(q, k_cmp, v_cmp, k_slc, v_slc, k_win, v_win, gates,
                  pos_k, w1_k, w2_k, pos_v, w1_v, w2_v, bias_table):
    B, S = q.shape[:2]
    G, HPG, Dh = NSA_GROUPS, NSA_HPG, HEAD_DIM
    scale = Dh ** -0.5
    kc = compress(k_cmp, pos_k, w1_k, w2_k)
    vc = compress(v_cmp, pos_v, w1_v, w2_v)
    n_cmp = kc.shape[1]
    cmp_start = CMP_STRIDE * jnp.arange(n_cmp)
    cmp_end = cmp_start + CMP_BLOCK - 1
    n_sel = S // SEL_BLOCK
    top_k = min(SEL_TOPK, n_sel)
    sel_idx = jnp.arange(n_sel)
    sel_start = SEL_BLOCK * sel_idx
    overlap = jnp.clip(jnp.minimum(cmp_start[:, None] + CMP_BLOCK, sel_start[None, :] + SEL_BLOCK)
                       - jnp.maximum(cmp_start[:, None], sel_start[None, :]), 0, None
                       ).astype(jnp.float32) / CMP_BLOCK
    k_slc_t = jnp.transpose(k_slc, (0, 2, 1, 3))
    v_slc_t = jnp.transpose(v_slc, (0, 2, 1, 3))
    pad = ((0, 0), (WINDOW, 0), (0, 0), (0, 0))
    k_win_p = jnp.pad(k_win, pad)
    v_win_p = jnp.pad(v_win, pad)
    bias_g = bias_table.astype(jnp.float32).reshape(NUM_BUCKETS, G, HPG)
    b_ix = jnp.arange(B)[:, None, None]
    g_ix = jnp.arange(G)[None, :, None]

    def block(i):
        q0 = i * QBLK
        t = q0 + jnp.arange(QBLK)
        qb = lax.dynamic_slice_in_dim(q, q0, QBLK, axis=1).reshape(B, QBLK, G, HPG, Dh)
        gb = lax.dynamic_slice_in_dim(gates, q0, QBLK, axis=1).reshape(B, QBLK, 3, G, HPG)
        s_c = jnp.einsum('bqghd,bngd->bghqn', qb, kc).astype(jnp.float32) * scale
        m_c = cmp_end[None, :] <= t[:, None]
        p_c = masked_softmax(s_c, m_c) * jnp.any(m_c, axis=-1)[:, None].astype(jnp.float32)
        o_c = jnp.einsum('bghqn,bngd->bqghd', p_c.astype(vc.dtype), vc)
        imp = jnp.einsum('bghqn,nj->bgqj', p_c, overlap)
        cur = t // SEL_BLOCK
        forced = ((sel_idx[None, :] == 0) | (sel_idx[None, :] == cur[:, None])
                  | (sel_idx[None, :] == cur[:, None] - 1))
        valid = sel_start[None, :] <= t[:, None]
        score = jnp.where(valid, imp + jnp.where(forced, SEL_FORCE, 0.0), NEG_INF)
        _, blk = lax.top_k(score, top_k)
        tok = (blk[..., None] * SEL_BLOCK + jnp.arange(SEL_BLOCK)).reshape(B, G, -1)
        ks = k_slc_t[b_ix, g_ix, tok].reshape(B, G, QBLK, top_k * SEL_BLOCK, Dh)
        vs = v_slc_t[b_ix, g_ix, tok].reshape(B, G, QBLK, top_k * SEL_BLOCK, Dh)
        rel_s = t[None, None, :, None] - tok.reshape(B, G, QBLK, top_k * SEL_BLOCK)
        b_s = jnp.moveaxis(bias_g[t5_bucket(rel_s), jnp.arange(G)[None, :, None, None]], -1, 2)
        s_s = jnp.einsum('bqghd,bgqkd->bghqk', qb, ks).astype(jnp.float32) * scale + b_s
        p_s = masked_softmax(s_s, (rel_s >= 0)[:, :, None])
        o_s = jnp.einsum('bghqk,bgqkd->bqghd', p_s.astype(vs.dtype), vs)
        kw = lax.dynamic_slice_in_dim(k_win_p, q0, WINDOW + QBLK, axis=1)
        vw = lax.dynamic_slice_in_dim(v_win_p, q0, WINDOW + QBLK, axis=1)
        s_pos = q0 - WINDOW + jnp.arange(WINDOW + QBLK)
        rel_w = t[:, None] - s_pos[None, :]
        m_w = (rel_w >= 0) & (rel_w < WINDOW) & (s_pos[None, :] >= 0)
        b_w = jnp.transpose(bias_g[t5_bucket(rel_w)], (2, 3, 0, 1))
        s_w = jnp.einsum('bqghd,bkgd->bghqk', qb, kw).astype(jnp.float32) * scale + b_w
        p_w = masked_softmax(s_w, m_w)
        o_w = jnp.einsum('bghqk,bkgd->bqghd', p_w.astype(vw.dtype), vw)
        o = (gb[:, :, 0, :, :, None] * o_c + gb[:, :, 1, :, :, None] * o_s
             + gb[:, :, 2, :, :, None] * o_w)
        return o.reshape(B, QBLK, G * HPG * Dh)

    out = lax.map(block, jnp.arange(S // QBLK))
    return jnp.moveaxis(out, 0, 1).reshape(B, S, G * HPG * Dh)

def hier_moe(h, wg, bg, we, be, w_gate, w_up, w_down):
    B, S, D = h.shape
    N = B * S
    xt = h.reshape(N, D)
    g_prob = jax.nn.softmax((xt @ wg).astype(jnp.float32) + bg.astype(jnp.float32), axis=-1)
    g_p, g_idx = lax.top_k(g_prob, 1)
    e_logits = ((xt @ we).astype(jnp.float32) + be.astype(jnp.float32)).reshape(N, N_GROUPS, EXPERTS_PER_GROUP)
    e_in = jnp.take_along_axis(e_logits, g_idx[:, :, None], axis=1)[:, 0]
    e_val, e_loc = lax.top_k(e_in, TOP_K_EXPERTS)
    weight = (g_p * jax.nn.softmax(e_val, axis=-1)).astype(h.dtype)
    eid = g_idx * EXPERTS_PER_GROUP + e_loc
    nk = N * TOP_K_EXPERTS
    flat_e = eid.reshape(-1)
    flat_w = weight.reshape(-1)
    flat_tok = jnp.repeat(jnp.arange(N), TOP_K_EXPERTS)
    order = jnp.argsort(flat_e)
    se, stok, sw = flat_e[order], flat_tok[order], flat_w[order]
    counts = jnp.bincount(flat_e, length=N_EXPERTS)
    start = jnp.cumsum(counts) - counts
    padded = (counts + MOE_CHUNK - 1) // MOE_CHUNK * MOE_CHUNK
    pend = jnp.cumsum(padded)
    dest = (pend - padded)[se] + jnp.arange(nk) - start[se]
    n_chunks = -(-nk // MOE_CHUNK) + N_EXPERTS
    P = n_chunks * MOE_CHUNK
    slot_tok = jnp.zeros((P,), jnp.int32).at[dest].set(stok)
    slot_w = jnp.zeros((P,), h.dtype).at[dest].set(sw)
    chunk_e = jnp.minimum(jnp.searchsorted(pend, jnp.arange(n_chunks) * MOE_CHUNK, side='right'),
                          N_EXPERTS - 1)
    xbuf = xt[slot_tok].reshape(n_chunks, MOE_CHUNK, D)

    def expert_chunk(args):
        xc, e = args
        return (jax.nn.silu(xc @ w_gate[e]) * (xc @ w_up[e])) @ w_down[e]

    ybuf = lax.map(expert_chunk, (xbuf, chunk_e)).reshape(P, D)
    y = jnp.zeros((N, D), h.dtype).at[slot_tok].add(ybuf * slot_w[:, None])
    return y.reshape(B, S, D)

def setup_inputs(seed: int = 0) -> dict:
    key = jax.random.key(seed)
    ks = jax.random.split(key, 24)

    def nrm(k, shape, scale):
        return jax.random.normal(k, shape, jnp.float32) * scale

    return {
        "x": nrm(ks[0], (BATCH, SEQ, D_MODEL), 1.0),
        "ln1": 1.0 + nrm(ks[1], (DEPTH, D_MODEL), 0.02),
        "w_in": nrm(ks[2], (DEPTH, D_MODEL, D_IN), D_MODEL ** -0.5),
        "diff_lambda": nrm(ks[3], (DEPTH, 4, HEAD_DIM), 0.1),
        "diff_subln": 1.0 + nrm(ks[4], (DEPTH, 2 * HEAD_DIM), 0.02),
        "fox_bf": 1.0 + 3.0 * jax.random.uniform(ks[5], (DEPTH, FOX_HEADS), jnp.float32),
        "cmp_pos_k": nrm(ks[6], (DEPTH, CMP_BLOCK, HEAD_DIM), 0.1),
        "cmp_w1_k": nrm(ks[7], (DEPTH, CMP_BLOCK * HEAD_DIM, CMP_HIDDEN), (CMP_BLOCK * HEAD_DIM) ** -0.5),
        "cmp_w2_k": nrm(ks[8], (DEPTH, CMP_HIDDEN, HEAD_DIM), CMP_HIDDEN ** -0.5),
        "cmp_pos_v": nrm(ks[9], (DEPTH, CMP_BLOCK, HEAD_DIM), 0.1),
        "cmp_w1_v": nrm(ks[10], (DEPTH, CMP_BLOCK * HEAD_DIM, CMP_HIDDEN), (CMP_BLOCK * HEAD_DIM) ** -0.5),
        "cmp_w2_v": nrm(ks[11], (DEPTH, CMP_HIDDEN, HEAD_DIM), CMP_HIDDEN ** -0.5),
        "t5_table": nrm(ks[12], (NUM_BUCKETS, DIFF_HEADS + NSA_HEADS), 0.5),
        "w_out": nrm(ks[13], (DEPTH, D_MIX, D_MODEL), D_MIX ** -0.5),
        "ln2": 1.0 + nrm(ks[14], (DEPTH, D_MODEL), 0.02),
        "router_group_w": nrm(ks[15], (DEPTH, D_MODEL, N_GROUPS), D_MODEL ** -0.5),
        "router_group_b": nrm(ks[16], (DEPTH, N_GROUPS), 0.01),
        "router_expert_w": nrm(ks[17], (DEPTH, D_MODEL, N_EXPERTS), D_MODEL ** -0.5),
        "router_expert_b": nrm(ks[18], (DEPTH, N_EXPERTS), 0.01),
        "w_gate": nrm(ks[19], (DEPTH, N_EXPERTS, D_MODEL, D_EXPERT), D_MODEL ** -0.5),
        "w_up": nrm(ks[20], (DEPTH, N_EXPERTS, D_MODEL, D_EXPERT), D_MODEL ** -0.5),
        "w_down": nrm(ks[21], (DEPTH, N_EXPERTS, D_EXPERT, D_MODEL), D_EXPERT ** -0.5),
        "ln_f": 1.0 + nrm(ks[22], (D_MODEL,), 0.02),
    }

def reference(x, ln1, w_in, diff_lambda, diff_subln, fox_bf, cmp_pos_k, cmp_w1_k, cmp_w2_k,
              cmp_pos_v, cmp_w1_v, cmp_w2_v, t5_table, w_out, ln2, router_group_w,
              router_group_b, router_expert_w, router_expert_b, w_gate, w_up, w_down, ln_f):
    B, S, _ = x.shape
    split_points = [int(v) for v in np.cumsum(SPLIT_SIZES)[:-1]]
    t5_a = t5_table[:, :DIFF_HEADS]
    t5_c = t5_table[:, DIFF_HEADS:]
    for l in range(DEPTH):
        h = rms_norm(x, ln1[l])
        proj = h @ w_in[l]
        (a_q, a_k, a_v, b_q, b_k, b_v, b_f, c_q, c_kc, c_vc, c_ks, c_vs, c_kw, c_vw,
         c_g) = jnp.split(proj, split_points, axis=-1)
        dl = diff_lambda[l].astype(jnp.float32)
        lam_init = 0.8 - 0.6 * math.exp(-0.3 * l)
        lam = jnp.exp(jnp.sum(dl[0] * dl[1])) - jnp.exp(jnp.sum(dl[2] * dl[3])) + lam_init
        o_a = diff_attention(a_q.reshape(B, S, DIFF_HEADS, 2, HEAD_DIM),
                             a_k.reshape(B, S, DIFF_HEADS, 2, HEAD_DIM),
                             a_v.reshape(B, S, DIFF_HEADS, 2 * HEAD_DIM), lam, t5_a)
        o_a = rms_norm(o_a, diff_subln[l]) * (1.0 - lam_init)
        o_b = forgetting_attention(b_q.reshape(B, S, FOX_HEADS, HEAD_DIM),
                                   b_k.reshape(B, S, FOX_HEADS, HEAD_DIM),
                                   b_v.reshape(B, S, FOX_HEADS, HEAD_DIM), b_f, fox_bf[l])
        kv_shape = (B, S, NSA_GROUPS, HEAD_DIM)
        o_c = nsa_attention(c_q.reshape(B, S, NSA_HEADS, HEAD_DIM),
                            c_kc.reshape(kv_shape), c_vc.reshape(kv_shape),
                            c_ks.reshape(kv_shape), c_vs.reshape(kv_shape),
                            c_kw.reshape(kv_shape), c_vw.reshape(kv_shape),
                            jax.nn.sigmoid(c_g.reshape(B, S, 3, NSA_HEADS)),
                            cmp_pos_k[l], cmp_w1_k[l], cmp_w2_k[l],
                            cmp_pos_v[l], cmp_w1_v[l], cmp_w2_v[l], t5_c)
        mix = jnp.concatenate([o_a.reshape(B, S, -1), o_b.reshape(B, S, -1), o_c], axis=-1)
        x = x + mix @ w_out[l]
        h = rms_norm(x, ln2[l])
        x = x + hier_moe(h, router_group_w[l], router_group_b[l], router_expert_w[l],
                         router_expert_b[l], w_gate[l], w_up[l], w_down[l])
    return rms_norm(x, ln_f)


_drawn_inputs = setup_inputs


def setup_inputs(seed=0):
    import zlib

    import numpy as np

    out = dict(_drawn_inputs(seed))
    spreads = {}
    factors = {'diff_lambda': 8.0,
     'diff_subln': 13.616,
     'cmp_pos_k': 42.181,
     'router_group_b': 16.552,
     'router_expert_b': 27.818,
     'ln_f': 7.974,
     'cmp_w1_k': 2.998,
     'cmp_w2_k': 2.75,
     'cmp_pos_v': 4.65,
     'ln2': 5.193}
    for name, (base, spread) in spreads.items():
        noise = np.random.default_rng([zlib.crc32(name.encode()), seed]).standard_normal(out[name].shape)
        drawn = base * np.exp(spread * noise) if base else spread * noise
        out[name] = __import__('jax').numpy.asarray(drawn.astype(out[name].dtype))
    for name, factor in factors.items():
        out[name] = (out[name] * factor).astype(out[name].dtype)
    return out
```

```python
import math
from contextlib import ExitStack

import numpy as np

import concourse.bass as bass
from concourse import mybir

F32 = mybir.dt.float32
F32R = mybir.dt.float32r
I32 = mybir.dt.int32
U32 = mybir.dt.uint32
ALU = mybir.AluOpType
ACT = mybir.ActivationFunctionType
AX_X = mybir.AxisListType.X

P = 128
D = 2048
T = 512
NT = T // P
KT = D // P
HD = 64
DIFF_HEADS = D // 4 // (2 * HD)
FOX_HEADS = D // 4 // HD
NSA_HEADS = D // 2 // HD
GROUPS = 4
CMP_BLOCK = 32
CMP_STRIDE = 16
CMP_HIDDEN = 256
N_CMP = (T - CMP_BLOCK) // CMP_STRIDE + 1
CMP_PAD = 32
SEL_BLOCK = 64
SEL_TOPK = 16
WINDOW = 512
BUCKETS = 32
MAX_DISTANCE = 128
N_GROUPS = 8
PER_GROUP = 8
E_ALL = N_GROUPS * PER_GROUP
D_EXPERT = D // 8
EPS = 1e-6
NEG = -1e30
LAM_INIT = 0.8 - 0.6 * math.exp(-0.3 * 0)
SCALE = HD ** -0.5
T5_HEADS = DIFF_HEADS + NSA_HEADS
assert min(SEL_TOPK, T // SEL_BLOCK) == T // SEL_BLOCK and WINDOW >= T

_SIZES = (512, 512, 512, 512, 512, 512, FOX_HEADS, 1024, 256, 256, 256, 256, 256, 256, 3 * NSA_HEADS)
(AQ, AK, AV, BQ, BK, BV, BF, CQ, CKC, CVC, CKS, CVS, CKW, CVW, CG) = [sum(_SIZES[:i]) for i in range(15)]
D_IN = sum(_SIZES)
MISC = FOX_HEADS + 3 * NSA_HEADS

C_IDENT = 0
C_TRI = C_IDENT + P
TRI_W = T + 3 * P
C_BUCKET = C_TRI + TRI_W
STRIP = 3 * P
C_CMASK = C_BUCKET + STRIP
C_CANY = C_CMASK + NT * CMP_PAD
C_DIAG = C_CANY + NT
C_IOTA = C_DIAG + P
C_TOK = C_IOTA + E_ALL
C_ALL = C_TOK + NT
N_SMALLS = 12

DIFF_STEPS = [("diff", 0, qb) for qb in range(NT)]
FOX_STEPS = [("fox", 0, qb) for qb in range(NT)]
NSA_STEPS = ([("cmp", 0, qb) for qb in range(NT)]
             + [(kind, pair, qb) for kind in ("slc", "win") for pair in range(2) for qb in range(NT)])
STEPS = {"diff": DIFF_STEPS, "fox": FOX_STEPS, "nsa": NSA_STEPS}
TILES = {"diff": [("q", 1), ("k", 2), ("v", 3)],
         "fox": [("q", 1), ("k", 2), ("v", 3)],
         "nsa": [("q0", 0), ("q1", 1), ("k", 2), ("v", 3)]}
UNITS = 4
assert DIFF_HEADS == UNITS and FOX_HEADS == 2 * UNITS and GROUPS == UNITS
SEGMENTS = [("diff", "fox"), ("fox", "nsa"), ("nsa", None)]
CREDIT = 2

CAP = 64
PASSES = T // CAP
PAIRS = E_ALL // 2
OUT_OF_RANGE = 4096


def constants():
    c = np.zeros((P, C_ALL), np.float32)
    p = np.arange(P)
    c[:, C_IDENT:C_IDENT + P] = np.eye(P, dtype=np.float32)
    c[:, C_TRI:C_TRI + TRI_W] = p[:, None] <= np.arange(TRI_W)[None, :] - 3 * P
    rel = 2 * P - 1 - np.arange(STRIP)
    half = BUCKETS // 2
    n = np.maximum(rel, 0)
    nf = np.maximum(n, half).astype(np.float32)
    large = half + (np.log(nf / np.float32(half)) / np.float32(math.log(MAX_DISTANCE / half))
                    * np.float32(BUCKETS - half)).astype(np.int32)
    bucket = np.where(n < half, n, np.minimum(large, BUCKETS - 1))
    strip = np.zeros((BUCKETS + 1, STRIP), np.float32)
    seen = rel >= 0
    strip[bucket[seen], np.arange(STRIP)[seen]] += 1.0
    strip[BUCKETS - 1, seen] -= 1.0
    strip[BUCKETS, ~seen] = 1.0
    c[:BUCKETS + 1, C_BUCKET:C_BUCKET + STRIP] = strip
    t = np.arange(T).reshape(NT, P)
    end = CMP_STRIDE * np.arange(CMP_PAD) + CMP_BLOCK - 1
    valid = (end[None, None, :] <= t[:, :, None]) & (np.arange(CMP_PAD) < N_CMP)
    c[:, C_CMASK:C_CANY] = np.where(valid, 0.0, NEG).transpose(1, 0, 2).reshape(P, -1)
    c[:, C_CANY:C_DIAG] = valid.any(-1).T
    c[:, C_DIAG:C_IOTA] = np.where(p[None, :] <= p[:, None], 0.0, NEG)
    c[:, C_IOTA:C_TOK] = np.arange(E_ALL)
    c[:, C_TOK:C_ALL] = t.T
    return c


class Chain:

    def __init__(self, eng, sem):
        self.eng, self.sem, self.base, self.reg, self.per, self.local = eng, sem, 0, None, 0, 0

    def loop(self, reg, per):
        self.reg, self.per, self.local = reg, per, 0

    def end(self, trips):
        assert self.local == self.per, (self.local, self.per)
        self.base += self.per * trips
        self.reg, self.local = None, 0

    def __call__(self, ins):
        ins.then_inc(self.sem, 1)
        self.local += 1
        if self.reg is None:
            self.base, self.local = self.base + 1, 0
            self.eng.wait_ge(self.sem, self.base)
        else:
            self.eng.wait_ge(self.sem, self.reg * self.per + (self.base + self.local))


class Fence:

    def __init__(self, eng, sem):
        self.eng, self.sem = eng, sem

    def __call__(self):
        self.eng.sem_inc(self.sem, 1)


def bcast(ap, axis, n):
    dims = [list(x) for x in ap.ap]
    return bass.AP(ap.tensor, ap.offset, dims[:axis] + [[0, n]] + dims[axis:])


def part(steps, tiles, s, second):
    for j in range(tiles):
        a, b = j * steps // tiles, (j + 1) * steps // tiles
        if a <= s < b:
            m, r = 2 * (b - a), 2 * (s - a) + second
            return j, KT * r // m, KT * (r + 1) // m
    return None


STEPS_BEFORE = {"diff": 0, "fox": 4 * UNITS, "nsa": 8 * UNITS}
UNITS_BEFORE = {"diff": 0, "fox": UNITS, "nsa": 2 * UNITS}
STAGED_BEFORE = {"diff": 0, "fox": 3 * UNITS, "nsa": 6 * UNITS}
PRE_TILES = 5
LANDED_BEFORE = {"diff": {1: 16, 2: 16, 3: 16},
                 "fox": {s: 16 * (1 + UNITS) for s in (1, 2, 3)},
                 "nsa": {0: 48, **{s: 16 * (1 + 2 * UNITS) for s in (1, 2, 3)}}}
LANDED_PER = {"diff": {1: 16, 2: 16, 3: 16}, "fox": {1: 16, 2: 16, 3: 16}, "nsa": {0: 16, 1: 16, 2: 32, 3: 32}}
LANDED_END = {s: LANDED_BEFORE["nsa"][s] + UNITS * LANDED_PER["nsa"][s] for s in range(4)}
ALL_TILES = PRE_TILES + 6 * UNITS + 4 * UNITS
LINKS = {"diff": 4 * 4, "fox": 4 * 3, "nsa": 4 * 5 + 16 * 4}
ALL_STEPS = 8 * UNITS + len(NSA_STEPS) * UNITS


def hybrid_block_moe_kernel(nc, x_in, ln1, w_in, diff_lambda, diff_subln, fox_bf, cmp_pos_k, cmp_w1_k,
                            cmp_w2_k, cmp_pos_v, cmp_w1_v, cmp_w2_v, t5_table, w_out, ln2,
                            router_group_w, router_group_b, router_expert_w, router_expert_b,
                            w_gate, w_up, w_down, ln_f, table, out):
    with ExitStack() as ctx:
        def sb(name, shape, dt=F32):
            return ctx.enter_context(nc.sbuf_tensor(name, shape, dt))

        def psum(name, shape):
            return ctx.enter_context(nc.psum_tensor(name, shape, F32))

        def sem(name):
            return ctx.enter_context(nc.semaphore(name))

        strip_dram = nc.dram_tensor("strip_scratch", [T5_HEADS, P * STRIP], F32, kind="Internal").ap()
        negc_dram = nc.dram_tensor("negc_scratch", [FOX_HEADS, T], F32, kind="Internal").ap()
        h2_dram = nc.dram_tensor("h2_scratch", [T, D], F32, kind="Internal").ap()
        slot_dram = nc.dram_tensor("slot_scratch", [T * E_ALL, 1], I32, kind="Internal").ap()
        y_dram = nc.dram_tensor("y_scratch", [2 * T, D], F32, kind="Internal").ap()

        KB = 256
        X0, HT0, MIX0, RING0, AT0, END = 0, 32 * KB, 64 * KB, 96 * KB, 128 * KB, 188 * KB
        arena, rounded = {}, {}
        for name, a, b in (("x", X0, HT0), ("ht", HT0, MIX0), ("mix", MIX0, RING0), ("ring", RING0, AT0), ("at", AT0, END)):
            place = -(-nc.sbuf_base // 32) * 32
            arena[a, b] = sb(f"{name}_region", [P, b - a])
            if name in ("ht", "ring", "at"):
                rounded[a, b] = nc.alloc_sbuf_tensor_at(f"{name}_rounded", [P, b - a], F32R, offset=place)

        def region(at, *shape, memory=arena):
            n = int(np.prod(shape))
            (a, whole), = [(a, t) for (a, b), t in memory.items() if a <= at and at + n <= b]
            flat = whole[:, at - a:at - a + n]
            if len(shape) == 1:
                return flat
            names = "abcd"[:len(shape)]
            return flat.rearrange(f"p ({' '.join(names)}) -> p {' '.join(names)}",
                                  **{k: v for k, v in zip(names[1:], shape[1:])})

        x_sb = region(X0, NT, D)
        hT = region(HT0, KT, T)
        mix = region(MIX0, NT, D)
        ring = [region(RING0 + s * 8 * KB, KT, P) for s in range(4)]
        ring_out = [region(RING0 + s * 8 * KB, 4, T) for s in range(4)]
        wo_high = [region(AT0 + (44 + s * 8) * KB, 4, T) for s in range(2)]
        wo_high_r = [region(AT0 + (44 + s * 8) * KB, 4, T, memory=rounded) for s in range(2)]
        wo_low_r = [region(RING0 + s * 8 * KB, 4, T, memory=rounded) for s in range(4)]
        mixT_high_r = region(HT0, KT, T, memory=rounded)
        mixT_low_r = region(AT0 + 12 * KB, KT, T, memory=rounded)
        h_rows = region(MIX0, NT, D)
        kv2 = region(MIX0, 2 * GROUPS, T)
        flat_kv = region(MIX0 + 16 * KB, 2, KT, GROUPS, N_CMP)
        negc = mix[:, :, D // 2:D].rearrange("p u (h t) -> p u h t", h=2)
        bias = region(AT0, T5_HEADS, 2 * P)
        st_q = [region(AT0 + (20 + 2 * j) * KB, T) for j in range(2)]
        st_k = region(AT0 + 24 * KB, T)
        st_v = region(AT0 + 26 * KB, NT, P)
        q_live = [region(AT0 + (28 + 2 * j) * KB, T) for j in range(2)]
        k_live = [region(AT0 + (32 + 2 * j) * KB, T) for j in range(2)]
        v_live = region(AT0 + 36 * KB, NT, P)
        probs = region(AT0 + 38 * KB, 2, 2, T)
        pT = region(AT0 + 46 * KB, 2, T)
        squares = region(AT0 + 50 * KB, DIFF_HEADS, 2 * HD)
        w1 = region(AT0 + 28 * KB, 2, KT, CMP_HIDDEN)
        ex_w = [AT0 + 12 * KB, HT0]
        ex_gu = [region(a, 2, KT * D_EXPERT) for a in ex_w]
        ex_down = [region(a + 32 * KB, 2, D) for a in ex_w]
        xg = [region(RING0 - 16 * KB + 8 * KB * b, D) for b in range(2)]
        y_sb = [region(RING0 + 8 * KB * b, D) for b in range(2)]
        xT = region(RING0 + 16 * KB, KT, CAP)
        silu = region(RING0 + 20 * KB, D_EXPERT)
        hid = region(RING0 + 21 * KB, D_EXPERT)
        hidT = region(RING0 + 22 * KB, 2, CAP)
        y_rows = [[region(HT0 + (2 * b + k) * 8 * KB, D) for k in range(2)] for b in range(2)]
        out_sb = [region(RING0 + 8 * KB * b, D) for b in range(2)]
        lnf_sb = region(RING0 + 24 * KB, D)
        h2_rows = mix
        ln2_sb = region(RING0 + 0 * KB, D)
        sq = [region(AT0 + (5 + 2 * j) * KB, T) for j in range(3)]
        rw_sb = region(AT0 + 0 * KB, KT, N_GROUPS + E_ALL)

        consts = sb("consts", [P, C_ALL])
        ident = consts[:, C_IDENT:C_IDENT + P]
        tri = consts[:, C_TRI:C_TRI + TRI_W]
        ones = consts[:, C_TRI + T:C_TRI + T + P]
        cmask = consts[:, C_CMASK:C_CANY].rearrange("p (q n) -> p q n", q=NT)
        diag = consts[:, C_DIAG:C_DIAG + P]
        iota = consts[:, C_IOTA:C_IOTA + E_ALL]
        small = sb("small", [P, 896])
        at = [0]

        def tiny(*shape):
            n = int(np.prod(shape))
            a = small[:, at[0]:at[0] + n]
            at[0] += n
            if len(shape) == 1:
                return a
            names = "abcd"[:len(shape)]
            return a.rearrange(f"p ({' '.join(names)}) -> p {' '.join(names)}",
                               **{k: v for k, v in zip(names[1:], shape[1:])})

        ln1_sb = tiny(KT)
        pos_sb = tiny(2, KT)
        subln_sb = tiny(2 * HD)
        bf_sb = tiny(FOX_HEADS)
        ss = tiny(NT)
        rstd = tiny(NT)
        neglam = tiny(1)
        lam2 = tiny(2)
        lam_e = tiny(2)
        cq = tiny(NT, FOX_HEADS)
        gates = tiny(NT, 3 * NSA_HEADS)
        nmx = tiny(2, 2)
        cmx = tiny(2, 2)
        rsum = tiny(2, 2)
        rinv = tiny(2, 2)
        csum = tiny(2, 2)
        coef = tiny(2, 2)
        ccoef = tiny(2, 2)
        dss = tiny(NT * DIFF_HEADS)
        drs = tiny(NT * DIFF_HEADS)
        ss2 = tiny(NT, NT)
        rb_sb = tiny(N_GROUPS + E_ALL)
        wts = tiny(2, NT)
        tab_sb = sb("tab_sb", [BUCKETS + 1, T5_HEADS])
        lam_sb = sb("lam_sb", [P, 4, HD])
        fg = sb("fg", [P, NT, MISC])
        fz = sb("fz", [P, 3, NT, FOX_HEADS])
        w2k_sb = sb("w2k_sb", [P, 2, 2, HD])
        w2v_sb = sb("w2v_sb", [P, 2, HD])
        kcT = sb("kcT", [P, GROUPS, CMP_PAD])
        kc_live = sb("kc_live", [P, CMP_PAD])
        vblk = region(AT0 + 52 * KB, GROUPS, 4 * HD)
        slot_i = sb("slot_i", [CAP, E_ALL], I32)
        slot_f = sb("slot_f", [CAP, 2, E_ALL])
        tok_i = sb("tok_i", [CAP, E_ALL], I32)
        g_idx = [sb(f"g_idx{b}", [CAP, 1], I32) for b in range(2)]
        s_idx = [sb(f"s_idx{b}", [CAP, 1], I32) for b in range(2)]
        most_i = sb("most_i", [P, 1], I32)
        count_i = sb("count_i", [P, E_ALL], I32)
        dest_i = sb("dest_i", [P, 2 * NT], I32)
        asg_i = sb("asg_i", [P, 2 * NT], I32)
        gl_x = region(MIX0, 2, 2, GROUPS * N_CMP)
        gl_a = region(MIX0 + 2 * KB, 2, 2, GROUPS * N_CMP)
        gl_h = region(MIX0 + 8 * KB, 2, 2, GROUPS * N_CMP)
        sq_last = region(RING0 + 16 * KB, D)
        logits = region(AT0 + 5 * KB, NT, N_GROUPS + E_ALL)
        e_log, top1, top2, cand, chosen = [region(AT0 + 6 * KB + KB // 4 + j * KB, NT, E_ALL) for j in range(5)]
        strip_sb = region(AT0 + 26 * KB, STRIP)
        negc_sb = region(AT0 + 22 * KB, T)

        S = psum("S", [P, 2, 2, T])
        PT = psum("PT", [P, 2, T])
        O = psum("O", [P, 2, 2, P])
        PJ = psum("PJ", [P, T])
        otmp = sb("otmp", [P, 2, HD])
        g_tmp = sb("g_tmp", [P, 6, NT, N_GROUPS])
        r_tmp = sb("r_tmp", [P, 12, NT])
        revi = sb("revi", [P, E_ALL])
        dest_f = sb("dest_f", [P, 2, NT])
        asg_f = sb("asg_f", [P, 2, NT])
        far_i = sb("far_i", [P, T * E_ALL // P], I32)

        consts_in, smalls_in, w1_in = sem("consts_in"), sem("smalls_in"), sem("w1_in")
        x_in_sem = [sem(f"x_tile_in{t}") for t in range(NT)]
        landed = [sem(f"ring{s}_landed") for s in range(4)]
        strip_ready, strip_copied, strip_stored = sem("strip_ready"), sem("strip_copied"), sem("strip_stored")
        bias_in, tab_ready = sem("bias_in"), sem("tab_ready")
        rows_ready, row_sum, rstd_ready = sem("rows_ready"), sem("row_sum"), sem("rstd_ready")
        ms_ready, root_ready = sem("ms_ready"), sem("root_ready")
        hT_transposed, hT_copied = sem("hT_transposed"), sem("hT_copied")
        projected, staged = sem("projected"), sem("staged")
        kv_copied_a, kv_copied_v = sem("kv_copied_a"), sem("kv_copied_v")
        flat_ready, hidden_ready = sem("flat_ready"), sem("hidden_ready")
        gelu_in, gelu_tanh, gelu_ready = sem("gelu_in"), sem("gelu_tanh"), sem("gelu_ready")
        kc_ready, cmp_ready = sem("kc_ready"), sem("cmp_ready")
        f_in, f_exp, f_log, logf_ready = sem("f_in"), sem("f_exp"), sem("f_log"), sem("logf_ready")
        g_exp, lam_ready, lam_exp = sem("g_exp"), sem("lam_ready"), sem("lam_exp")
        cum_ready, cum_copied_a, cum_copied_v, negc_stored, negc_in = (
            sem("cum_ready"), sem("cum_copied_a"), sem("cum_copied_v"), sem("negc_stored"),
                                                       sem("negc_in"))
        live_qk, live_v = sem("live_qk"), sem("live_v")
        scores_ready, max_ready, exp_done, cmp_normed = (sem("scores_ready"), sem("max_ready"), sem("exp_done"),
                                                         sem("cmp_normed"))
        transposed, pT_copied_a, pT_copied_v = sem("transposed"), sem("pT_copied_a"), sem("pT_copied_v")
        outs_ready, out_done = sem("outs_ready"), sem("out_done")
        mix_ready, mix_transposed, mix_copied_a, mix_copied_v = (sem("mix_ready"), sem("mix_transposed"),
                                                                 sem("mix_copied_a"), sem("mix_copied_v"))
        wo_rounded, wo_split = sem("wo_rounded"), sem("wo_split")
        wo_used, wo_ready, wo_added = sem("wo_used"), sem("wo_ready"), sem("wo_added")
        ln2_in, rw_in = sem("ln2_in"), sem("rw_in")
        row2_sum, rows2_ready = sem("row2_sum"), sem("rows2_ready")
        h2_stored, h2_transposed, h2_copied = sem("h2_stored"), sem("h2_transposed"), sem("h2_copied")
        logits_ready, g_max, g_exped, e_diff, e_exped = (sem("logits_ready"), sem("g_max"), sem("g_exped"),
                                                         sem("e_diff"), sem("e_exped"))
        chosen_ready, ranks_ready, most_ready, dest_ready = (sem("chosen_ready"), sem("ranks_ready"),
                                                             sem("most_ready"), sem("dest_ready"))
        far_ready, far_stored, slots_stored, slots_in, slots_ready = (
            sem("far_ready"), sem("far_stored"), sem("slots_stored"), sem("slots_in"), sem("slots_ready"))
        xg_cleared, g_copied, s_copied = sem("xg_cleared"), sem("g_copied"), sem("s_copied")
        gathered = [sem(f"gathered{b}") for b in range(2)]
        scattered = [sem(f"scattered{b}") for b in range(2)]
        gu_in = [sem(f"gu_in{b}") for b in range(2)]
        down_in = [sem(f"down_in{b}") for b in range(2)]
        xg_transposed, xT_a, xT_v = sem("xg_transposed"), sem("xT_a"), sem("xT_v")
        gu_done, silu_done, hid_done = sem("gu_done"), sem("silu_done"), sem("hid_done")
        hid_transposed, hidT_done, down_done = sem("hid_transposed"), sem("hidT_done"), sem("down_done")
        y_a, y_v = sem("y_a"), sem("y_v")
        pass_in, pass_ready = sem("pass_in"), sem("pass_ready")
        y_in = [sem(f"y_in{b}") for b in range(2)]
        lnf_in, y_added, f_sum, f_out, out_stored = (sem("lnf_in"), sem("y_added"), sem("f_sum"), sem("f_out"),
                                                     [sem(f"out_stored{b}") for b in range(2)])
        pe_fence, pool_fence = sem("pe_fence"), sem("pool_fence")
        dve_chain, end_chain = sem("dve_chain"), sem("end_chain")

        w_cols = w_in[0].rearrange("(p k) n -> p k n", k=KT)
        wo_rows = w_out[0].rearrange("(c k p) n -> p c k n", p=P, k=4)
        gate_rows = w_gate[0].rearrange("e (p k) n -> p e (k n)", k=KT)
        up_rows = w_up[0].rearrange("e (p k) n -> p e (k n)", k=KT)
        down_rows = w_down[0].rearrange("e (p k) n -> p e (k n)", k=2)
        x_rows = x_in[0].rearrange("(t p) d -> p t d", p=P)
        out_rows = out[0].rearrange("(t p) d -> p t d", p=P)
        slot_rows = slot_dram.rearrange("(r e) a -> r (e a)", e=E_ALL)

        def wo_wait(eng, m, c):
            if c < 3:
                eng.wait_ge(wo_used, 3 * m + c + 1)
            else:
                eng.wait_ge(wo_ready, NT * (m + 1))

        def row_to_all(ap, offset, n):
            return bass.AP(ap.tensor, offset, [[0, P], [1, n]])

        block = ctx.enter_context(nc.Block())

        @block.sync
        def _(sp):
            sp.dma_start(consts[:], table).then_inc(consts_in, 16)
            for t in range(NT):
                sp.dma_start(x_sb[:, t, :], x_rows[:, t, :]).then_inc(x_in_sem[t], 16)
            smalls = [
                (ln1_sb, ln1[0].rearrange("(p k) -> p k", k=KT)),
                (tab_sb[0:BUCKETS, :], t5_table),
                (bf_sb, row_to_all(fox_bf, 0, FOX_HEADS)),
                (lam_sb[:].rearrange("p a b -> p (a b)"), row_to_all(diff_lambda, 0, 4 * HD)),
                (subln_sb, row_to_all(diff_subln, 0, 2 * HD)),
                (w2k_sb[:, :, 0, :], cmp_w2_k[0].rearrange("(h p) d -> p h d", p=P)),
                (w2k_sb[:, :, 1, :], cmp_w2_k[0].rearrange("(h p) d -> p h d", p=P)),
                (w2v_sb[:], cmp_w2_v[0].rearrange("(h p) d -> p h d", p=P)),
                (rb_sb[:, 0:N_GROUPS], row_to_all(router_group_b, 0, N_GROUPS)),
                (rb_sb[:, N_GROUPS:], row_to_all(router_expert_b, 0, E_ALL)),
                (pos_sb[:, 0, :], cmp_pos_k[0].rearrange("(k l) d -> (l d) k", l=2)),
                (pos_sb[:, 1, :], cmp_pos_v[0].rearrange("(k l) d -> (l d) k", l=2)),
            ]
            assert len(smalls) == N_SMALLS
            with nc.allow_non_contiguous_dma("small tables"):
                for dst, src in smalls:
                    sp.dma_start(dst, src).then_inc(smalls_in, 16)

            def load(slot, *pieces):
                at = 0
                for col, n in pieces:
                    sp.dma_start(ring[slot][:, :, at:at + n], w_cols[:, :, bass.ds(col, n)]).then_inc(landed[slot], 16)
                    at += n

            load(0, (BF, FOX_HEADS), (CG, 3 * NSA_HEADS))
            load(1, (CKC, P))
            load(2, (CKC + P, P))
            load(3, (CVC, P))
            sp.dma_start(w1[:, 0, :, :], cmp_w1_k[0].rearrange("(k p) n -> p k n", p=P)).then_inc(w1_in, 16)
            sp.dma_start(w1[:, 1, :, :], cmp_w1_v[0].rearrange("(k p) n -> p k n", p=P)).then_inc(w1_in, 16)
            sp.wait_ge(projected, 1)
            load(0, (CVC + P, P))

            def load_unit(kind, u, reuse):
                for j, (name, slot) in enumerate(TILES[kind]):
                    sp.wait_ge(projected, reuse(j))
                    if kind == "diff":
                        load(slot, ({"q": AQ, "k": AK, "v": AV}[name] + u * P, P))
                    elif kind == "fox":
                        load(slot, ({"q": BQ, "k": BK, "v": BV}[name] + u * P, P))
                    elif name in ("q0", "q1"):
                        load(slot, (CQ + u * 2 * P + j * P, P))
                    else:
                        a, b = (CKS, CKW) if name == "k" else (CVS, CVW)
                        load(slot, (a + u * HD, HD), (b + u * HD, HD))

            load_unit("diff", 0, lambda j: 2 + j)
            sp.wait_ge(strip_copied, 1)
            sp.dma_start(strip_dram.rearrange("h (q n) -> h q n", q=P), bcast(strip_sb[0:T5_HEADS, :], 1, P))\
              .then_inc(strip_stored, 16)
            sp.wait_ge(strip_stored, 16)
            sp.dma_start(bias, bass.AP(strip_dram.tensor, P - 1, [[STRIP - 1, P], [P * STRIP, T5_HEADS], [1, 2 * P]]))\
              .then_inc(bias_in, 16)
            load_unit("diff", 1, lambda j: PRE_TILES + 1 + j)
            sp.wait_ge(cum_copied_a, 1)
            sp.dma_start(negc_dram, negc_sb[0:FOX_HEADS, :]).then_inc(negc_stored, 16)
            sp.wait_ge(negc_stored, 16)
            sp.wait_ge(cmp_ready, 1)
            for u in range(UNITS):
                sp.dma_start(negc[:, u, :, :], bass.AP(negc_dram.tensor, 2 * u * T, [[0, P], [T, 2], [1, T]]))\
                  .then_inc(negc_in, 16)
            with sp.Fori(2, UNITS) as u:
                load_unit("diff", u, lambda j: u * 3 + (PRE_TILES + j - 2))
            with sp.Fori(0, UNITS) as u:
                load_unit("fox", u, lambda j: u * 3 + (PRE_TILES + 3 * UNITS + j - 2))
            load_unit("nsa", 0, lambda j: PRE_TILES if j == 0 else PRE_TILES + 6 * UNITS - 3 + j)
            with sp.Fori(1, UNITS) as u:
                load_unit("nsa", u, lambda j: u * 4 + (PRE_TILES + 6 * UNITS + j - 3))
            for m in range(NT):
                for c in range(4):
                    if m == 0:
                        sp.wait_ge(projected, ALL_TILES - 3 + c)
                    else:
                        wo_wait(sp, m - 1, c)
                    sp.dma_start(ring_out[c], wo_rows[:, c, :, m * T:(m + 1) * T]).then_inc(landed[c], 16)
            sp.wait_ge(out_done, ALL_STEPS + CREDIT)
            rw_w = [(rw_sb[:, :, 0:N_GROUPS], router_group_w), (rw_sb[:, :, N_GROUPS:], router_expert_w)]
            with nc.allow_non_contiguous_dma("router weights"):
                for dst, src in rw_w:
                    sp.dma_start(dst, src[0].rearrange("(k p) n -> p k n", p=P)).then_inc(rw_in, 16)

            def load_expert(e, b):
                sp.dma_start(ex_gu[b][:, 0, :], gate_rows[:, e, :]).then_inc(gu_in[b], 16)
                sp.dma_start(ex_gu[b][:, 1, :], up_rows[:, e, :]).then_inc(gu_in[b], 16)
                sp.dma_start(ex_down[b].rearrange("p k n -> p (k n)"), down_rows[:, e, :]).then_inc(down_in[b], 16)

            sp.wait_ge(wo_ready, NT * NT)
            sp.dma_start(ln2_sb, row_to_all(ln2, 0, D)).then_inc(ln2_in, 16)
            load_expert(0, 0)
            for t in range(NT):
                sp.wait_ge(rows2_ready, t + 1)
                sp.dma_start(h2_dram[t * P:(t + 1) * P, :], h2_rows[:, t, :]).then_inc(h2_stored, 16)
            sp.wait_ge(h2_stored, 16 * NT)
            sp.wait_ge(logits_ready, 1)
            load_expert(1, 1)

            def expert_loads(c):
                with sp.Fori(0, PAIRS - 1) as i:
                    for b in range(2):
                        e = c * E_ALL + i * 2 + b
                        sp.wait_ge(gu_done, e + 1)
                        nxt = bass.ds(i * 2 + (b + 2), 1)
                        sp.dma_start(ex_gu[b][:, 0:1, :], gate_rows[:, nxt, :]).then_inc(gu_in[b], 16)
                        sp.dma_start(ex_gu[b][:, 1:2, :], up_rows[:, nxt, :]).then_inc(gu_in[b], 16)
                        sp.wait_ge(down_done, e + 1)
                        sp.dma_start(ex_down[b].rearrange("p k (a n) -> p a (k n)", a=1), down_rows[:, nxt, :])\
                          .then_inc(down_in[b], 16)

            expert_loads(0)
            sp.wait_ge(most_ready, 1)
            most = sp.value_load(most_i[0:1, 0:1], min_val=0, max_val=T)
            with sp.If(most > CAP):
                with sp.Fori(1, PASSES) as c:
                    sp.wait_ge(down_done, c * E_ALL)
                    sp.wait_ge(s_copied, c * E_ALL)
                    sp.wait_ge(g_copied, c * E_ALL)
                    load_expert(0, 0)
                    load_expert(1, 1)
                    sp.dma_start(slot_i[:], slot_rows[bass.ds(c * CAP, CAP), :]).then_inc(pass_in, 16)
                    expert_loads(c)
                sp.wait_ge(down_done, E_ALL * PASSES)
                for b in range(2):
                    sp.wait_ge(scattered[b], 16 * PAIRS * PASSES)
            with sp.Else():
                sp.wait_ge(down_done, E_ALL)
                for b in range(2):
                    sp.wait_ge(scattered[b], 16 * PAIRS)
            sp.dma_start(lnf_sb, row_to_all(ln_f, 0, D)).then_inc(lnf_in, 16)
            for t in range(NT):
                if t >= 2:
                    sp.wait_ge(y_added, t)
                for k in range(2):
                    sp.dma_start(y_rows[t % 2][k], y_dram[k * T + t * P:k * T + (t + 1) * P, :])\
                      .then_inc(y_in[t % 2], 16)
            for t in range(NT):
                sp.wait_ge(f_out, t + 1)
                sp.dma_start(out_rows[:, t, :], out_sb[t % 2]).then_inc(out_stored[t % 2], 16)
            for b in range(2):
                sp.wait_ge(out_stored[b], 16 * NT // 2)

        @block.gpsimd
        def _(pool):
            fence = Fence(pool, pool_fence)
            nc.gpsimd.memset(far_i[:], OUT_OF_RANGE).then_inc(far_ready, 1)
            pool.wait_ge(far_ready, 1)
            pool.dma_start(slot_dram.rearrange("(p n) a -> p (n a)", p=P), far_i[:]).then_inc(far_stored, 16)
            pool.wait_ge(far_stored, 16)
            pool.wait_ge(h2_stored, 16 * NT)
            pool.wait_ge(h2_copied, 4 * NT)
            for b in range(2):
                ins = nc.gpsimd.memset(xg[b][0:CAP, :], 0.0)
            ins.then_inc(xg_cleared, 1)
            pool.wait_ge(xg_cleared, 1)
            pool.wait_ge(dest_ready, 1)
            for j in range(2 * NT):
                pool.indirect_dma_start(slot_dram, bass.IndirectOffsetOnAxis(ap=dest_i[:, j:j + 1].bitcast(U32), axis=0),
                                        asg_i[:, j:j + 1], None,
                                        bounds_check=T * E_ALL - 1, oob_is_err=False).then_inc(slots_stored, 16)
            pool.wait_ge(slots_stored, 16 * 2 * NT)
            pool.dma_start(slot_i[:], slot_rows[0:CAP, :]).then_inc(slots_in, 16)

            def gather(col, count, b):
                pool.wait_ge(gathered[b], count * 16)
                fence()
                nc.gpsimd.tensor_copy(g_idx[b][:], tok_i[:, col]).then_inc(g_copied, 1)

            def by_rows(col, c, send):
                count = pool.value_load(count_i[0:1, col], min_val=0, max_val=T)
                with pool.If(count > c * CAP + CAP // 2):
                    send(CAP)
                with pool.Else():
                    send(CAP // 2)

            def start_gather(col, c, total, b):
                pool.wait_ge(g_copied, total)
                fence()
                by_rows(col, c, lambda n: pool.indirect_dma_start(
                    xg[b][0:n, :], None, h2_dram,
                    bass.IndirectOffsetOnAxis(ap=g_idx[b][0:n, :].bitcast(U32), axis=0),
                    bounds_check=T - 1, oob_is_err=False).then_inc(gathered[b], 16))

            def start_scatter(col, c, b):
                by_rows(col, c, lambda n: pool.indirect_dma_start(
                    y_dram, bass.IndirectOffsetOnAxis(ap=s_idx[b][0:n, :].bitcast(U32), axis=0),
                    y_sb[b][0:n, :], None, bounds_check=2 * T - 1, oob_is_err=False).then_inc(scattered[b], 16))

            def pair(c, i, last):
                for b in range(2):
                    e = c * E_ALL + i * 2 + b
                    k = c * PAIRS + i
                    if not (last and b == 1):
                        nxt = bass.ds(i * 2 + (b + 1), 1)
                        gather(nxt, k + b, 1 - b)
                        pool.wait_ge(xg_transposed, e)
                        start_gather(nxt, c, e + 2, 1 - b)
                    pool.wait_ge(scattered[b], k * 16)
                    fence()
                    nc.gpsimd.tensor_copy(s_idx[b][:], slot_i[:, bass.ds(i * 2 + b, 1)]).then_inc(s_copied, 1)
                    pool.wait_ge(s_copied, e + 1)
                    pool.wait_ge(y_a, e + 1)
                    pool.wait_ge(y_v, e + 1)
                    fence()
                    start_scatter(bass.ds(i * 2 + b, 1), c, b)

            def expert_rows(c):
                gather(bass.ds(0, 1), c * PAIRS, 0)
                pool.wait_ge(xg_transposed, c * E_ALL)
                start_gather(bass.ds(0, 1), c, c * E_ALL + 1, 0)
                pair(c, 0, False)
                with pool.Fori(1, PAIRS - 1) as i:
                    pair(c, i, False)
                pair(c, PAIRS - 1, True)

            pool.wait_ge(slots_ready, 1)
            pool.wait_ge(most_ready, 1)
            expert_rows(0)
            most = pool.value_load(most_i[0:1, 0:1], min_val=0, max_val=T)
            with pool.If(most > CAP):
                with pool.Fori(1, PASSES) as c:
                    pool.wait_ge(pass_ready, c)
                    expert_rows(c)
            with pool.Else():
                pool.wait_ge(most_ready, 1)

        @block.tensor
        def _(pe):
            mm = nc.tensor.matmul
            fence = Fence(pe, pe_fence)
            pe.sem_inc(transposed, CREDIT)
            pe.wait_ge(consts_in, 16)
            for t in range(NT):
                pe.wait_ge(rows_ready, t + 1)
                for j in range(4):
                    g = 4 * t + j
                    if g >= 2:
                        pe.wait_ge(hT_copied, g - 1)
                    for i in range(4):
                        k = 4 * j + i
                        ins = nc.tensor.transpose(PT[:, g % 2, i * P:(i + 1) * P], h_rows[:, t, k:D:KT], ident)
                    ins.then_inc(hT_transposed, 1)
            pe.wait_ge(smalls_in, 16 * N_SMALLS)
            pe.wait_ge(tab_ready, 1)
            Oflat = O[:].rearrange("p a b c -> p (a b c)")
            mm(Oflat[0:T5_HEADS, 0:STRIP], tab_sb[:], consts[0:BUCKETS + 1, C_BUCKET:C_BUCKET + STRIP],
               start=True, stop=True).then_inc(strip_ready, 1)
            pe.wait_ge(hT_copied, 4 * NT)

            pe.wait_ge(landed[0], 32)
            for t in range(NT):
                for k in range(KT):
                    ins = mm(PJ[:, t * MISC:(t + 1) * MISC], hT[:, k, t * P:(t + 1) * P], ring[0][:, k, 0:MISC],
                             start=k == 0, stop=k == KT - 1)
            ins.then_inc(projected, 1)
            for j, slot in enumerate((1, 2, 3, 0)):
                pe.wait_ge(landed[slot], 16 if slot else 48)
                for k in range(KT):
                    ins = mm(S[:, j // 2, j % 2, :], ring[slot][:, k, :], hT[:, k, :], start=k == 0, stop=k == KT - 1)
                ins.then_inc(projected, 1)

            def project(kind, u, j, lo, hi):
                name, slot = TILES[kind][j]
                n = len(TILES[kind])
                if lo == 0:
                    pe.wait_ge(landed[slot], u * LANDED_PER[kind][slot]
                               + (LANDED_BEFORE[kind][slot] + LANDED_PER[kind][slot]))
                    pe.wait_ge(staged, u * n + (STAGED_BEFORE[kind] + j + 1))
                if name == "v":
                    for i in range(4 * lo, 4 * hi):
                        t, k = i // KT, i % KT
                        ins = mm(PJ[:, t * P:(t + 1) * P], hT[:, k, t * P:(t + 1) * P], ring[slot][:, k, :],
                                 start=k == 0, stop=k == KT - 1)
                else:
                    for k in range(lo, hi):
                        ins = mm(PJ[:], ring[slot][:, k, :], hT[:, k, :], start=k == 0, stop=k == KT - 1)
                if hi == KT:
                    ins.then_inc(projected, 1)

            for j in range(3):
                project("diff", 0, j, 0, KT)

            pe.wait_ge(logf_ready, 1)
            for t in range(NT):
                for i in range(t + 1):
                    ins = mm(PT[:, 0, t * FOX_HEADS:(t + 1) * FOX_HEADS], tri[:, 3 * P:4 * P] if i == t else ones,
                             fz[:, 2, i, :], start=i == 0, stop=i == t)
            for i in range(NT):
                ins = mm(PT[0:FOX_HEADS, 1, :], fz[:, 2, i, :], tri[:, (3 - i) * P:(3 - i) * P + T],
                         start=i == 0, stop=i == NT - 1)
            ins.then_inc(cum_ready, 1)

            pe.wait_ge(flat_ready, 1)
            pe.wait_ge(w1_in, 32)
            H = S[:, 0, 0, 0:4 * GROUPS * N_CMP].rearrange("p (a n) -> p a n", a=4)
            for a in range(4):
                kv, half = a // 2, a % 2
                for k in range(KT):
                    ins = mm(H[:, a, :], w1[:, kv, k, half * P:(half + 1) * P],
                             flat_kv[:, kv, k, :, :].rearrange("p g n -> p (g n)"), start=k == 0, stop=k == KT - 1)
            ins.then_inc(hidden_ready, 1)
            pe.wait_ge(gelu_ready, 1)
            for half in range(2):
                ins = mm(S[:, 0, 1, 0:GROUPS * N_CMP], w2k_sb[:, half, :, :].rearrange("p a d -> p (a d)"),
                         gl_h[:, 0, half, :], start=half == 0, stop=half == 1)
            for g in range(GROUPS):
                for half in range(2):
                    ins = mm(S[0:N_CMP, 1, 0, g * HD:(g + 1) * HD], gl_h[:, 1, half, g * N_CMP:(g + 1) * N_CMP],
                             w2v_sb[:, half, :], start=half == 0, stop=half == 1)
            ins.then_inc(kc_ready, 1)
            pe.wait_ge(cmp_ready, 1)
            pe.wait_ge(cum_copied_a, 1)
            pe.wait_ge(cum_copied_v, 1)

            def scores(kind, u, pr, qb, par):
                for half in range(2):
                    rows = slice(half * HD, (half + 1) * HD)
                    cols = slice(qb * P, (qb + 1) * P)
                    if kind == "cmp":
                        for p2 in range(2):
                            ins = mm(S[:, par, half, p2 * CMP_PAD:(p2 + 1) * CMP_PAD], q_live[p2][rows, cols],
                                     kc_live[rows, :], start=True, stop=True)
                    else:
                        W = (qb + 1) * P
                        keys = k_live[1] if kind == "win" else k_live[0]
                        ins = mm(S[:, par, half, 0:W], q_live[pr][rows, cols], keys[rows, 0:W], start=True, stop=True)
                ins.then_inc(scores_ready, 1)

            def transpose_probs(kind, qb, par, n, cmp_n):
                pe.wait_ge(exp_done, n + (1 + CREDIT))
                if kind == "cmp":
                    pe.wait_ge(cmp_normed, cmp_n)
                    ins = nc.tensor.transpose(PT[:, 0, 0:P], probs[:, par, 0, 0:P], ident)
                else:
                    for half in range(2):
                        for kb in range(qb + 1):
                            ins = nc.tensor.transpose(PT[:, half, kb * P:(kb + 1) * P],
                                                      probs[:, par, half, kb * P:(kb + 1) * P], ident)
                ins.then_inc(transposed, 1)

            def values(kind, u, pr, qb, par, n):
                pe.wait_ge(pT_copied_a, n + 1)
                pe.wait_ge(pT_copied_v, n + 1)
                pe.wait_ge(out_done, n + CREDIT)
                if kind == "cmp":
                    ins = mm(O[:, par, :, :].rearrange("p a b -> p (a b)"), pT[:, 0, 0:P],
                             vblk[:, bass.ds(u, 1), :].rearrange("p a n -> p (a n)"), start=True, stop=True)
                else:
                    for half in range(2):
                        cols = {"diff": slice(0, P), "fox": slice(half * HD, (half + 1) * HD),
                                "slc": slice(0, HD), "win": slice(HD, P)}[kind]
                        w = cols.stop - cols.start
                        for kb in range(qb + 1):
                            ins = mm(O[:, par, half, 0:w], pT[:, half, kb * P:(kb + 1) * P], v_live[:, kb, cols],
                                     start=kb == 0, stop=kb == qb)
                ins.then_inc(outs_ready, 1)

            def unit(seg, u, nkind, nu):
                steps = STEPS[seg]
                n0 = u * len(steps) + STEPS_BEFORE[seg]
                gone = u + (UNITS_BEFORE[seg] + 1)

                def next_part(s, second):
                    if nkind is not None:
                        j, lo, hi = part(len(steps), len(TILES[nkind]), s, second)
                        if hi > lo:
                            project(nkind, nu, j, lo, hi)

                def cmp_at(s):
                    return u * NT + (s + 1)

                for s, (kind, pr, qb) in enumerate(steps):
                    if s == 0:
                        pe.wait_ge(live_qk, gone)
                    pe.wait_ge(exp_done, n0 + (s + 1))
                    scores(kind, u, pr, qb, s % 2)
                    next_part(s, 0)
                    if s > 0:
                        transpose_probs(steps[s - 1][0], steps[s - 1][2], (s - 1) % 2, n0 + (s - 1), cmp_at(s - 1))
                    next_part(s, 1)
                    if s == 1:
                        pe.wait_ge(live_v, gone)
                    if s > 0:
                        values(steps[s - 1][0], u, steps[s - 1][1], steps[s - 1][2], (s - 1) % 2, n0 + (s - 1))
                s = len(steps) - 1
                kind, pr, qb = steps[s]
                transpose_probs(kind, qb, s % 2, n0 + s, cmp_at(s))
                values(kind, u, pr, qb, s % 2, n0 + s)

            for seg, after in SEGMENTS:
                with pe.Fori(0, UNITS - 1) as u:
                    unit(seg, u, seg, u + 1)
                unit(seg, UNITS - 1, after, 0)

            def turn_tile(rows, t, signal, copied):
                for j in range(4):
                    g = 4 * t + j
                    if g >= 4:
                        pe.wait_ge(copied, g - 3)
                    for i in range(4):
                        k = 4 * j + i
                        ins = nc.tensor.transpose(S[:, g // 2 % 2, g % 2, i * P:(i + 1) * P],
                                                  rows[:, t, k * P:(k + 1) * P], ident)
                    ins.then_inc(signal, 1)

            pe.wait_ge(mix_ready, 1)
            for t in range(NT):
                turn_tile(mix, t, mix_transposed, mix_copied_v)
            pe.wait_ge(mix_copied_v, 4 * NT)

            for m in range(NT):
                for c in range(4):
                    pe.wait_ge(wo_split, 4 * m + c + 1)
                    w_hi, w_lo = wo_high_r[c % 2], wo_low_r[c]
                    for t in range(NT):
                        if c == 0 and m >= 1:
                            pe.wait_ge(wo_added, NT * (m - 1) + t + 1)
                        for i in range(4):
                            for n, (a, b) in enumerate(((mixT_high_r, w_hi), (mixT_high_r, w_lo), (mixT_low_r, w_hi))):
                                ins = mm(S[:, t // 2, t % 2, :], a[:, 4 * c + i, t * P:(t + 1) * P],
                                         b[:, i, :], start=c == 0 and i == 0 and n == 0,
                                         stop=c == 3 and i == 3 and n == 2)
                        if c == 3:
                            ins.then_inc(wo_ready, 1)
                    if c < 3:
                        ins.then_inc(wo_used, 1)

            R = N_GROUPS + E_ALL
            pe.wait_ge(rw_in, 32)
            for t in range(NT + 1):
                if t < NT:
                    pe.wait_ge(rows2_ready, t + 1)
                    turn_tile(h2_rows, t, h2_transposed, h2_copied)
                if t > 0:
                    pe.wait_ge(h2_copied, 4 * t)
                    for k in range(KT):
                        ins = mm(PJ[:, (t - 1) * R:t * R], hT[:, k, (t - 1) * P:t * P], rw_sb[:, k, :],
                                 start=k == 0, stop=k == KT - 1)
            ins.then_inc(logits_ready, 1)
            pe.wait_ge(chosen_ready, 1)
            for t in range(NT):
                for i in range(t + 1):
                    ins = mm(Oflat[:, t * E_ALL:(t + 1) * E_ALL], tri[:, 3 * P - 1:4 * P - 1] if i == t else ones,
                             chosen[:, i, :], start=i == 0, stop=i == t)
            for i in range(NT):
                ins = mm(PT[:, 0, 0:E_ALL], ones, chosen[:, i, :], start=i == 0, stop=i == NT - 1)
            ins.then_inc(ranks_ready, 1)

            Y = S[:, 1, :, :]
            GU = PJ

            def turn_gathered(e, k, b):
                pe.wait_ge(gathered[b], k * 16 + 16)
                pe.wait_ge(xT_a, e)
                pe.wait_ge(xT_v, e)
                fence()
                for j in range(KT):
                    ins = nc.tensor.transpose(PT[:, j // 8, (j % 8) * CAP:(j % 8 + 1) * CAP],
                                              xg[b][0:CAP, j:D:KT], ident[0:CAP, 0:CAP])
                ins.then_inc(xg_transposed, 1)

            def expert(c, i, b, last):
                e = c * E_ALL + i * 2 + b
                k = c * PAIRS + i
                gate = ex_gu[b][:, 0, :].rearrange("p (k n) -> p k n", k=KT)
                up = ex_gu[b][:, 1, :].rearrange("p (k n) -> p k n", k=KT)
                pe.wait_ge(gu_in[b], k * 32 + 32)
                pe.wait_ge(xT_a, e + 1)
                pe.wait_ge(xT_v, e + 1)
                pe.wait_ge(hid_done, e)
                for j in range(KT):
                    mm(GU[0:CAP, 0:D_EXPERT], xT[:, j, :], gate[:, j, :], start=j == 0, stop=j == KT - 1)
                    ins = mm(GU[CAP:2 * CAP, 0:D_EXPERT], xT[:, j, :], up[:, j, :], start=j == 0, stop=j == KT - 1)
                ins.then_inc(gu_done, 1)
                if not (last and b == 1):
                    turn_gathered(e + 1, k + b, 1 - b)
                pe.wait_ge(hid_done, e + 1)
                pe.wait_ge(hidT_done, e)
                fence()
                for j in range(2):
                    ins = nc.tensor.transpose(Oflat[:, j * CAP:(j + 1) * CAP], hid[0:CAP, j:D_EXPERT:2],
                                              ident[0:CAP, 0:CAP])
                ins.then_inc(hid_transposed, 1)
                pe.wait_ge(hidT_done, e + 1)
                pe.wait_ge(down_in[b], k * 16 + 16)
                pe.wait_ge(y_a, e)
                pe.wait_ge(y_v, e)
                for m in range(2):
                    for j in range(2):
                        for side in range(2):
                            ins = mm(Y[side * CAP:(side + 1) * CAP, m, :], hidT[:, j, :],
                                     ex_down[b][:, j, (2 * side + m) * T:(2 * side + m + 1) * T],
                                     start=j == 0, stop=j == 1)
                ins.then_inc(down_done, 1)

            def expert_pass(c):
                turn_gathered(c * E_ALL, c * PAIRS, 0)
                for b in range(2):
                    expert(c, 0, b, False)
                with pe.Fori(1, PAIRS - 1) as i:
                    for b in range(2):
                        expert(c, i, b, False)
                for b in range(2):
                    expert(c, PAIRS - 1, b, True)

            pe.wait_ge(dest_ready, 1)
            expert_pass(0)
            pe.wait_ge(most_ready, 1)
            most = pe.value_load(most_i[0:1, 0:1], min_val=0, max_val=T)
            with pe.If(most > CAP):
                with pe.Fori(1, PASSES) as c:
                    expert_pass(c)
            with pe.Else():
                pe.wait_ge(most_ready, 1)

        @block.scalar
        def _(act):
            fn = nc.scalar.activation
            act.sem_inc(exp_done, CREDIT)

            def root(of, count):
                act.wait_ge(ms_ready, count)
                fn(of, of, ACT.Sqrt).then_inc(root_ready, 1)

            Oflat = O[:].rearrange("p a b c -> p (a b c)")
            for t in range(NT):
                act.wait_ge(x_in_sem[t], 16)
                fn(h_rows[:, t, :], x_sb[:, t, :], ACT.Square, accum_out=ss[:, t:t + 1]).then_inc(row_sum, 1)
                act.wait_ge(row_sum, t + 1)
                root(ss[:, t:t + 1], t + 1)
                act.wait_ge(rstd_ready, t + 1)
                fn(h_rows[:, t, :], x_sb[:, t, :], ACT.Identity, scale=rstd[:, t:t + 1]).then_inc(rows_ready, 1)
            act.wait_ge(strip_ready, 1)
            fn(strip_sb[0:T5_HEADS, :], Oflat[0:T5_HEADS, 0:STRIP], ACT.Copy).then_inc(strip_copied, 1)
            act.wait_ge(projected, 1)
            fn(fg[:].rearrange("p t n -> p (t n)"), PJ[:, 0:NT * MISC], ACT.Copy).then_inc(staged, 1)
            act.wait_ge(staged, 1)
            fn(gates, fg[:, :, FOX_HEADS:], ACT.Exp, scale=-1.0).then_inc(g_exp, 1)
            act.wait_ge(lam_ready, 1)
            fn(lam_e, lam2, ACT.Exp).then_inc(lam_exp, 1)
            act.wait_ge(f_in, 1)
            fn(fz[:, 1], fz[:, 0], ACT.Abs).then_inc(f_exp, 1)
            act.wait_ge(f_exp, 1)
            fn(fz[:, 1], fz[:, 1], ACT.Exp, scale=-1.0).then_inc(f_exp, 1)
            act.wait_ge(f_exp, 2)
            fn(fz[:, 1], fz[:, 1], ACT.Ln, bias=1.0).then_inc(f_log, 1)
            for j in range(4):
                act.wait_ge(projected, 2 + j)
                for e in range(2):
                    ins = fn(kv2[0:HD, 2 * j + e, :], S[e * HD:(e + 1) * HD, j // 2, j % 2, :], ACT.Copy)
                ins.then_inc(kv_copied_a, 1)

            def stage(kind, u, j, first=False):
                name, n = TILES[kind][j][0], len(TILES[kind])
                act.wait_ge(projected, u * n + (PRE_TILES + STAGED_BEFORE[kind] + j + 1))
                if not first:
                    act.wait_ge(live_v if name == "v" else live_qk, u + UNITS_BEFORE[kind])
                if name == "v":
                    ins = fn(st_v.rearrange("p t n -> p (t n)"), PJ[:], ACT.Copy)
                elif name == "k":
                    ins = fn(st_k, PJ[:], ACT.Copy)
                else:
                    ins = fn(st_q[1 if name == "q1" else 0], PJ[:], ACT.Copy, scale=SCALE)
                ins.then_inc(staged, 1)

            act.wait_ge(strip_stored, 16)
            for j in range(3):
                stage("diff", 0, j, first=True)
            act.wait_ge(cum_ready, 1)
            fn(negc_sb[0:FOX_HEADS, :], PT[0:FOX_HEADS, 1, :], ACT.Copy, scale=-1.0).then_inc(cum_copied_a, 1)
            act.wait_ge(gelu_in, 1)
            fn(gl_a, gl_a, ACT.Tanh, scale=math.sqrt(2 / math.pi)).then_inc(gelu_tanh, 1)
            act.wait_ge(hidden_ready, 1)
            act.wait_ge(staged, 4)
            fn(v_live, st_v, ACT.Copy).then_inc(live_v, 1)
            act.wait_ge(negc_stored, 16)

            def exps(kind, qb, par, n):
                act.wait_ge(max_ready, n + 1)
                act.wait_ge(transposed, n + 1)
                act.wait_ge(out_done, n + 1)
                if kind == "cmp":
                    ins = fn(probs[:, par, 0, 0:P].rearrange("p (h n) -> p h n", h=2), S[:, par, :, 0:2 * CMP_PAD],
                             ACT.Exp)
                else:
                    for half in range(2):
                        ins = fn(probs[:, par, half, 0:(qb + 1) * P], S[:, par, half, 0:(qb + 1) * P], ACT.Exp,
                                 bias=nmx[:, par, half:half + 1], accum_out=rsum[:, par, half:half + 1])
                ins.then_inc(exp_done, 1)

            def copy_pT(kind, qb, n):
                act.wait_ge(transposed, n + (1 + CREDIT))
                w = P if kind == "cmp" else (qb + 1) * P
                fn(pT[:, 0, 0:w], PT[:, 0, 0:w], ACT.Copy).then_inc(pT_copied_a, 1)

            def unit(seg, u, nkind, nu):
                steps = STEPS[seg]
                n0 = u * len(steps) + STEPS_BEFORE[seg]
                for s, (kind, pr, qb) in enumerate(steps):
                    exps(kind, qb, s % 2, n0 + s)
                    if s > 0:
                        copy_pT(steps[s - 1][0], steps[s - 1][2], n0 + (s - 1))
                    if nkind is not None:
                        j, lo, hi = part(len(steps), len(TILES[nkind]), s, 1)
                        if hi == KT:
                            stage(nkind, nu, j)
                copy_pT(steps[-1][0], steps[-1][2], n0 + (len(steps) - 1))
                if nkind is not None:
                    act.wait_ge(outs_ready, n0 + len(steps))
                    act.wait_ge(staged, nu * len(TILES[nkind]) + (STAGED_BEFORE[nkind] + len(TILES[nkind]) + 1))
                    fn(v_live, st_v, ACT.Copy).then_inc(live_v, 1)

            for seg, after in SEGMENTS:
                with act.Fori(0, UNITS - 1) as u:
                    unit(seg, u, seg, u + 1)
                unit(seg, UNITS - 1, after, 0)
                if seg == "fox":
                    root(dss, NT + 1)

            for g in range(4 * NT):
                t, j = g // 4, g % 4
                act.wait_ge(mix_transposed, g + 1)
                fn(mixT_high_r[:, 4 * j:4 * j + 4, t * P:(t + 1) * P],
                   S[:, g // 2 % 2, g % 2, :].rearrange("p (a b) -> p a b", a=4), ACT.Copy).then_inc(mix_copied_a, 1)
            def round_wo(n):
                act.wait_ge(landed[n % 4], LANDED_END[n % 4] + 16 * (n // 4 + 1))
                if n >= 2:
                    wo_wait(act, (n - 2) // 4, (n - 2) % 4)
                fn(wo_high_r[n % 2], ring_out[n % 4], ACT.Copy).then_inc(wo_rounded, 1)

            for n in range(5):
                round_wo(n)
            for m in range(NT):
                for t in range(NT):
                    act.wait_ge(wo_added, NT * m + t + 1)
                    n = NT * m + t
                    if n >= 3:
                        act.wait_ge(row2_sum, n - 2)
                    fn(sq[n % 3], x_sb[:, t, m * T:(m + 1) * T], ACT.Square, accum_out=ss2[:, t, m:m + 1])\
                        .then_inc(row2_sum, 1)
                for n in range(4 * m + 5, min(4 * m + 9, 4 * NT)):
                    round_wo(n)
            root(ss, NT + 2)
            for g in range(4 * NT):
                t, j = g // 4, g % 4
                act.wait_ge(h2_transposed, g + 1)
                fn(hT[:, 4 * j:4 * j + 4, t * P:(t + 1) * P],
                   S[:, g // 2 % 2, g % 2, :].rearrange("p (a b) -> p a b", a=4), ACT.Copy).then_inc(h2_copied, 1)
            act.wait_ge(g_max, 1)
            fn(g_tmp[:, 1], g_tmp[:, 0], ACT.Exp).then_inc(g_exped, 1)
            act.wait_ge(e_diff, 1)
            fn(r_tmp[:, 4], r_tmp[:, 3], ACT.Exp).then_inc(e_exped, 1)

            def copy_xT(e):
                act.wait_ge(xg_transposed, e + 1)
                fn(xT[:, 0:KT // 2, :], PT[:, 0, :].rearrange("p (a b) -> p a b", a=KT // 2), ACT.Copy)\
                    .then_inc(xT_a, 1)

            def expert(c, i, b, last):
                e = c * E_ALL + i * 2 + b
                k = c * PAIRS + i
                act.wait_ge(gu_done, e + 1)
                act.wait_ge(hid_done, e)
                fn(silu[0:CAP, :], PJ[0:CAP, 0:D_EXPERT], ACT.Silu).then_inc(silu_done, 1)
                if not (last and b == 1):
                    copy_xT(e + 1)
                act.wait_ge(down_done, e + 1)
                act.wait_ge(scattered[b], k * 16)
                fn(y_sb[b][0:CAP, 0:D // 2].rearrange("p (m n) -> p m n", m=2), S[0:CAP, 1, :, :], ACT.Copy)\
                    .then_inc(y_a, 1)

            def expert_pass(c):
                copy_xT(c * E_ALL)
                for b in range(2):
                    expert(c, 0, b, False)
                with act.Fori(1, PAIRS - 1) as i:
                    for b in range(2):
                        expert(c, i, b, False)
                for b in range(2):
                    expert(c, PAIRS - 1, b, True)

            expert_pass(0)
            act.wait_ge(most_ready, 1)
            most = act.value_load(most_i[0:1, 0:1], min_val=0, max_val=T)
            with act.If(most > CAP):
                with act.Fori(1, PASSES) as c:
                    expert_pass(c)
            with act.Else():
                act.wait_ge(most_ready, 1)
            for t in range(NT):
                act.wait_ge(y_added, t + 1)
                fn(sq_last, x_sb[:, t, :], ACT.Square, accum_out=ss[:, t:t + 1]).then_inc(f_sum, 1)
                root(ss[:, t:t + 1], NT + 3 + t)

        @block.vector
        def _(dve):
            v = nc.vector
            link = Chain(dve, dve_chain)
            dve.sem_inc(out_done, CREDIT)
            Oflat = O[:].rearrange("p a b c -> p (a b c)")
            v.memset(tab_sb[BUCKETS:BUCKETS + 1, :], NEG).then_inc(tab_ready, 1)
            link(v.memset(kcT[:], 0.0))

            def inverse_rms(t, count):
                v.tensor_scalar(ss[:, t:t + 1], ss[:, t:t + 1], 1.0 / D, EPS, ALU.mult, ALU.add).then_inc(ms_ready, 1)
                dve.wait_ge(root_ready, count)
                return v.reciprocal(rstd[:, t:t + 1], ss[:, t:t + 1])

            for t in range(NT):
                dve.wait_ge(row_sum, t + 1)
                inverse_rms(t, t + 1).then_inc(rstd_ready, 1)
            dve.wait_ge(consts_in, 16)
            dve.wait_ge(smalls_in, 16 * N_SMALLS)
            link(v.tensor_tensor(otmp[:], lam_sb[:, 0:4:2, :], lam_sb[:, 1:4:2, :], ALU.mult))
            v.tensor_reduce(lam2, otmp[:], AX_X, ALU.add).then_inc(lam_ready, 1)
            for g in range(4 * NT):
                t, j = g // 4, g % 4
                dve.wait_ge(hT_transposed, g + 1)
                v.tensor_tensor(hT[:, 4 * j:4 * j + 4, t * P:(t + 1) * P],
                                PT[:, g % 2, :].rearrange("p (a b) -> p a b", a=4),
                                bcast(ln1_sb[:, 4 * j:4 * j + 4], 2, P), ALU.mult).then_inc(hT_copied, 1)
            dve.wait_ge(lam_exp, 1)
            link(v.tensor_scalar(neglam, lam_e[:, 1:2], -LAM_INIT, None, ALU.add))
            link(v.tensor_tensor(neglam, neglam, lam_e[:, 0:1], ALU.subtract))
            link(v.tensor_scalar(subln_sb, subln_sb, 1.0 - LAM_INIT, None, ALU.mult))
            link(v.tensor_scalar(revi[:], iota, -1.0, float(E_ALL), ALU.mult, ALU.add))
            dve.wait_ge(staged, 1)
            v.tensor_tensor(fz[:, 0], fg[:, :, 0:FOX_HEADS], bcast(bf_sb, 1, NT), ALU.add).then_inc(f_in, 1)
            dve.wait_ge(f_log, 1)
            v.scalar_tensor_tensor(fz[:, 2], fz[:, 0], 0.0, fz[:, 1], ALU.min, ALU.subtract).then_inc(logf_ready, 1)
            dve.wait_ge(g_exp, 1)
            link(v.tensor_scalar(gates, gates, 1.0, None, ALU.add))
            link(v.reciprocal(gates, gates))
            for j in range(4):
                dve.wait_ge(kv_copied_a, 1 + j)
                for e in range(2):
                    ins = v.tensor_copy(kv2[HD:P, 2 * j + e, 0:T - 1], S[e * HD:(e + 1) * HD, j // 2, j % 2, 1:T])
                ins.then_inc(kv_copied_v, 1)
            dve.wait_ge(kv_copied_a, 4)
            dve.wait_ge(kv_copied_v, 4)
            for kv in range(2):
                for k in range(KT):
                    ins = v.tensor_scalar(flat_kv[:, kv, k, :, :],
                                          kv2[:, kv * GROUPS:(kv + 1) * GROUPS, 2 * k:2 * k + CMP_STRIDE * (N_CMP - 1) + 1:CMP_STRIDE],
                                          pos_sb[:, kv, k:k + 1], None, ALU.add)
            ins.then_inc(flat_ready, 1)
            dve.wait_ge(cum_ready, 1)
            v.tensor_copy(cq, PT[:, 0, 0:NT * FOX_HEADS].rearrange("p (t h) -> p t h", t=NT)).then_inc(cum_copied_v, 1)
            dve.wait_ge(hidden_ready, 1)
            H = S[:, 0, 0, 0:4 * GROUPS * N_CMP].rearrange("p (a b n) -> p a b n", a=2, b=2)
            link(v.memset(vblk, 0.0))
            link(v.tensor_copy(gl_x, H))
            link(v.tensor_tensor(gl_a, gl_x, gl_x, ALU.mult))
            link(v.tensor_scalar(gl_a, gl_a, 0.044715, 1.0, ALU.mult, ALU.add))
            v.tensor_tensor(gl_a, gl_a, gl_x, ALU.mult).then_inc(gelu_in, 1)
            dve.wait_ge(gelu_tanh, 1)
            link(v.scalar_tensor_tensor(gl_h, gl_a, 1.0, gl_x, ALU.add, ALU.mult))
            v.tensor_scalar(gl_h, gl_h, 0.5, None, ALU.mult).then_inc(gelu_ready, 1)
            dve.wait_ge(kc_ready, 1)
            v.tensor_copy(kcT[:, :, 0:N_CMP], S[:, 0, 1, 0:GROUPS * N_CMP].rearrange("p (g n) -> p g n", g=GROUPS))
            for half in range(2):
                for p2 in range(2):
                    r, col = (half * 2 + p2) * CMP_PAD, (p2 * 2 + half) * HD
                    ins = v.tensor_copy(vblk[r:r + N_CMP, :, col:col + HD],
                                        S[0:N_CMP, 1, 0, 0:GROUPS * HD].rearrange("p (g d) -> p g d", g=GROUPS))
            ins.then_inc(cmp_ready, 1)

            def go_live(kind, u):
                js = [name for name, _ in TILES[kind]].index("k")
                dve.wait_ge(staged, u * len(TILES[kind]) + (STAGED_BEFORE[kind] + js + 2))
                if kind == "nsa":
                    v.tensor_copy(kc_live[:].rearrange("p (a n) -> p a n", a=1), kcT[:, bass.ds(u, 1), :])
                    for p2 in range(2):
                        v.tensor_copy(q_live[p2], st_q[p2])
                    for half in range(2):
                        for which in range(2):
                            ins = v.tensor_copy(k_live[which][half * HD:(half + 1) * HD, :],
                                                st_k[which * HD:(which + 1) * HD, :])
                else:
                    v.tensor_copy(q_live[0], st_q[0])
                    ins = v.tensor_copy(k_live[0], st_k)
                ins.then_inc(live_qk, 1)

            go_live("diff", 0)
            dve.wait_ge(bias_in, 16)

            def row_max(kind, u, pr, qb, par, n):
                dve.wait_ge(scores_ready, n + 1)
                W = (qb + 1) * P
                if kind == "cmp":
                    sc = S[:, par, :, 0:2 * CMP_PAD].rearrange("p h (u n) -> p h u n", u=2)
                    link(v.tensor_tensor(sc, sc, bcast(bcast(cmask[:, qb, :], 1, 2), 1, 2), ALU.add))
                    link(v.tensor_reduce(cmx, sc, AX_X, ALU.max))
                    v.tensor_tensor(sc, sc, bcast(cmx, 3, CMP_PAD), ALU.subtract).then_inc(max_ready, 1)
                    return
                if kind == "fox":
                    for half in range(2):
                        sc = S[:, par, half, 0:W]
                        ins = v.scalar_tensor_tensor(sc, sc, cq[:, qb, bass.ds(u * 2 + half, 1)],
                                                     negc[:, bass.ds(u, 1), half, 0:W].rearrange("p a t -> p (a t)"),
                                                     ALU.add, ALU.add)
                    link(ins)
                    sc = S[:, par, :, qb * P:W]
                    link(v.tensor_tensor(sc, sc, bcast(diag, 1, 2), ALU.add))
                else:
                    near = min(W, 2 * P)
                    sc = S[:, par, :, W - near:W]
                    if kind == "diff":
                        b = bias[:, bass.ds(u, 1), 2 * P - near:2 * P].broadcast_to([P, 2, near])
                    else:
                        b = bias[:, bass.ds(u * 4 + (DIFF_HEADS + pr * 2), 2), 2 * P - near:2 * P]
                    link(v.tensor_tensor(sc, sc, b, ALU.add))
                v.tensor_reduce(nmx[:, par, :], S[:, par, :, 0:W], AX_X, ALU.max, negate=True).then_inc(max_ready, 1)

            def normalise_cmp(u, qb, par, n):
                dve.wait_ge(exp_done, n + (1 + CREDIT))
                pr4 = probs[:, par, 0, 0:P].rearrange("p (h u n) -> p h u n", h=2, u=2)
                link(v.tensor_reduce(csum, pr4, AX_X, ALU.add))
                g4 = gates[:, qb, bass.ds(u * 4, 4)].rearrange("p (u h) -> p h u", h=2)
                link(v.reciprocal(csum, csum))
                link(v.scalar_tensor_tensor(ccoef, g4, consts[:, C_CANY + qb:C_CANY + qb + 1], csum,
                                            ALU.mult, ALU.mult))
                v.tensor_tensor(pr4, pr4, bcast(ccoef, 3, CMP_PAD), ALU.mult).then_inc(cmp_normed, 1)

            def copy_pT(kind, qb, n):
                dve.wait_ge(transposed, n + (1 + CREDIT))
                if kind == "cmp":
                    dve.sem_inc(pT_copied_v, 1)
                else:
                    v.tensor_copy(pT[:, 1, 0:(qb + 1) * P], PT[:, 1, 0:(qb + 1) * P]).then_inc(pT_copied_v, 1)

            def outputs(kind, u, pr, qb, par, n):
                dve.wait_ge(outs_ready, n + 1)
                if kind == "cmp":
                    ins = v.tensor_copy(mix[:, qb, bass.ds(u * 4 * HD + D // 2, 4 * HD)],
                                        O[:, par, :, :].rearrange("p a b -> p (a b)"))
                elif kind == "diff":
                    m = mix[:, qb, bass.ds(u * P, P)]
                    link(v.reciprocal(rinv[:, par, :], rsum[:, par, :]))
                    link(v.tensor_tensor(coef[:, par, 0:1], neglam, rinv[:, par, 1:2], ALU.mult))
                    link(v.tensor_scalar(m, O[:, par, 0, :], rinv[:, par, 0:1], None, ALU.mult))
                    ins = v.scalar_tensor_tensor(m, O[:, par, 1, :], coef[:, par, 0:1], m, ALU.mult, ALU.add)
                elif kind == "fox":
                    m = mix[:, qb, bass.ds(u * P + D // 4, P)].rearrange("p (h d) -> p h d", h=2)
                    link(v.reciprocal(rinv[:, par, :], rsum[:, par, :]))
                    ins = v.tensor_tensor(m, O[:, par, :, 0:HD], bcast(rinv[:, par, :], 2, HD), ALU.mult)
                else:
                    m = mix[:, qb, bass.ds(u * 4 * HD + (D // 2 + pr * P), P)].rearrange("p (h d) -> p h d", h=2)
                    which = NSA_HEADS * (1 if kind == "slc" else 2)
                    link(v.reciprocal(rinv[:, par, :], rsum[:, par, :]))
                    link(v.tensor_tensor(coef[:, par, :], gates[:, qb, bass.ds(u * 4 + (which + pr * 2), 2)],
                                         rinv[:, par, :], ALU.mult))
                    link(v.tensor_tensor(otmp[:], O[:, par, :, 0:HD], bcast(coef[:, par, :], 2, HD), ALU.mult))
                    ins = v.tensor_tensor(m, m, otmp[:], ALU.add)
                ins.then_inc(out_done, 1)

            def unit(seg, u, nkind, nu):
                steps = STEPS[seg]
                n0 = u * len(steps) + STEPS_BEFORE[seg]
                last = len(steps) - 1
                for s, (kind, pr, qb) in enumerate(steps):
                    row_max(kind, u, pr, qb, s % 2, n0 + s)
                    if s > 0:
                        copy_pT(steps[s - 1][0], steps[s - 1][2], n0 + (s - 1))
                    if kind == "cmp":
                        normalise_cmp(u, qb, s % 2, n0 + s)
                    if s > 0:
                        outputs(steps[s - 1][0], u, steps[s - 1][1], steps[s - 1][2], (s - 1) % 2, n0 + (s - 1))
                if nkind is not None:
                    go_live(nkind, nu)
                copy_pT(steps[last][0], steps[last][2], n0 + last)
                outputs(steps[last][0], u, steps[last][1], steps[last][2], last % 2, n0 + last)

            for seg, after in SEGMENTS:
                if seg == "fox":
                    dve.wait_ge(negc_in, 16 * UNITS)
                links = LINKS[seg]
                with dve.Fori(0, UNITS - 1) as u:
                    link.loop(u, links)
                    unit(seg, u, seg, u + 1)
                link.end(UNITS - 1)
                unit(seg, UNITS - 1, after, 0)
                if seg == "fox":
                    md = mix[:, :, 0:D // 4].rearrange("p t (h d) -> p t h d", h=DIFF_HEADS)
                    dsq = squares
                    dve.wait_ge(out_done, STEPS_BEFORE["nsa"] + CREDIT)
                    for t in range(NT):
                        link(v.tensor_tensor(dsq, md[:, t], md[:, t], ALU.mult))
                        link(v.tensor_reduce(dss[:, t * 4:(t + 1) * 4], dsq, AX_X, ALU.add))
                    v.tensor_scalar(dss, dss, 1.0 / (2 * HD), EPS, ALU.mult, ALU.add).then_inc(ms_ready, 1)
                    dve.wait_ge(root_ready, NT + 1)
                    link(v.reciprocal(drs, dss))
                    for t in range(NT):
                        link(v.tensor_tensor(md[:, t], md[:, t], bcast(drs[:, t * 4:(t + 1) * 4], 2, 2 * HD), ALU.mult))
                        link(v.tensor_tensor(md[:, t], md[:, t], bcast(subln_sb, 1, DIFF_HEADS), ALU.mult))
            dve.wait_ge(out_done, ALL_STEPS + CREDIT)
            dve.sem_inc(mix_ready, 1)

            for g in range(4 * NT):
                t, j = g // 4, g % 4
                dve.wait_ge(mix_copied_a, g + 1)
                cols = (slice(None), slice(4 * j, 4 * j + 4), slice(t * P, (t + 1) * P))
                v.tensor_tensor(mixT_low_r[cols], S[:, g // 2 % 2, g % 2, :].rearrange("p (a b) -> p a b", a=4), mixT_high_r[cols].bitcast(F32),
                                ALU.subtract).then_inc(mix_copied_v, 1)
            def split_wo(n):
                dve.wait_ge(wo_rounded, n + 1)
                v.tensor_tensor(wo_low_r[n % 4], ring_out[n % 4], wo_high_r[n % 2].bitcast(F32), ALU.subtract)\
                 .then_inc(wo_split, 1)

            for n in range(5):
                split_wo(n)
            for m in range(NT):
                for t in range(NT):
                    dve.wait_ge(wo_ready, NT * m + t + 1)
                    xs = x_sb[:, t, m * T:(m + 1) * T]
                    v.tensor_tensor(xs, xs, S[:, t // 2, t % 2, :], ALU.add).then_inc(wo_added, 1)
                for n in range(4 * m + 5, min(4 * m + 9, 4 * NT)):
                    split_wo(n)
            dve.wait_ge(row2_sum, NT * NT)
            link(v.tensor_reduce(ss, ss2, AX_X, ALU.add))
            v.tensor_scalar(ss, ss, 1.0 / D, EPS, ALU.mult, ALU.add).then_inc(ms_ready, 1)
            dve.wait_ge(root_ready, NT + 2)
            link(v.reciprocal(rstd, ss))
            dve.wait_ge(ln2_in, 16)
            for t in range(NT):
                v.scalar_tensor_tensor(h2_rows[:, t, :], x_sb[:, t, :], rstd[:, t:t + 1], ln2_sb, ALU.mult, ALU.mult)\
                 .then_inc(rows2_ready, 1)

            dve.wait_ge(logits_ready, 1)
            R = N_GROUPS + E_ALL
            link(v.tensor_tensor(logits, PJ[:, 0:NT * R].rearrange("p (t r) -> p t r", t=NT),
                                 bcast(rb_sb, 1, NT), ALU.add))
            g_log, e_all = logits[:, :, 0:N_GROUPS], logits[:, :, N_GROUPS:]
            g_m, g_sum, g_c, d12, ex, v1, v2, one_e, p_g, c1 = [r_tmp[:, j] for j in (0, 1, 2, 3, 4, 5, 6, 7, 8, 9)]

            def first_max(onehot, vals, best, cands, order, tmp, n):
                link(v.tensor_reduce(best, vals, AX_X, ALU.max))
                link(v.tensor_tensor(cands, vals, bcast(best, 2, n), ALU.is_equal))
                link(v.tensor_tensor(cands, cands, bcast(order, 1, NT), ALU.mult))
                link(v.tensor_reduce(tmp, cands, AX_X, ALU.max))
                link(v.tensor_tensor(onehot, cands, bcast(tmp, 2, n), ALU.is_equal))

            g_hot = g_tmp[:, 3]
            first_max(g_hot, g_log, g_m, g_tmp[:, 2], revi[:, 0:N_GROUPS], g_c, N_GROUPS)
            v.tensor_tensor(g_tmp[:, 0], g_log, bcast(g_m, 2, N_GROUPS), ALU.subtract).then_inc(g_max, 1)
            link(v.tensor_scalar(g_tmp[:, 4], g_hot, -1.0, -NEG, ALU.add, ALU.mult))
            el4 = e_log.rearrange("p t (g e) -> p t g e", g=N_GROUPS)
            for t in range(NT):
                link(v.tensor_tensor(el4[:, t], e_all[:, t, :].rearrange("p (g e) -> p g e", g=N_GROUPS),
                                     bcast(g_hot[:, t, :], 2, PER_GROUP), ALU.mult))
                link(v.tensor_tensor(el4[:, t], el4[:, t], bcast(g_tmp[:, 4, t, :], 2, PER_GROUP), ALU.add))
            first_max(top1, e_log, v1, cand, revi[:], c1, E_ALL)
            link(v.scalar_tensor_tensor(e_log, top1, NEG, e_log, ALU.mult, ALU.add))
            first_max(top2, e_log, v2, cand, revi[:], c1, E_ALL)
            v.tensor_tensor(d12, v2, v1, ALU.subtract).then_inc(e_diff, 1)
            v.tensor_tensor(chosen, top1, top2, ALU.add).then_inc(chosen_ready, 1)
            dve.wait_ge(g_exped, 1)
            link(v.tensor_reduce(g_sum, g_tmp[:, 1], AX_X, ALU.add))
            dve.wait_ge(e_exped, 1)
            link(v.tensor_scalar(one_e, ex, 1.0, None, ALU.add))
            link(v.tensor_tensor(one_e, one_e, g_sum, ALU.mult))
            link(v.reciprocal(wts[:, 0, :], one_e))
            link(v.tensor_tensor(wts[:, 1, :], wts[:, 0, :], ex, ALU.mult))
            dve.wait_ge(ranks_ready, 1)
            link(v.tensor_reduce(p_g[:, 0:1], PT[:, 0, 0:E_ALL], AX_X, ALU.max))
            v.tensor_copy(count_i[:], PT[:, 0, 0:E_ALL])
            v.tensor_copy(most_i[:], p_g[:, 0:1]).then_inc(most_ready, 1)
            link(v.scalar_tensor_tensor(cand, Oflat[:, 0:NT * E_ALL].rearrange("p (t e) -> p t e", t=NT),
                                        float(E_ALL), bcast(iota, 1, NT), ALU.mult, ALU.add))
            for k, hot in enumerate((top1, top2)):
                link(v.tensor_tensor(e_log, hot, cand, ALU.mult))
                link(v.tensor_reduce(dest_f[:, k, :], e_log, AX_X, ALU.add))
                link(v.tensor_scalar(asg_f[:, k, :], consts[:, C_TOK:C_ALL], float(k * T), None, ALU.add))
            link(v.tensor_copy(dest_i[:].rearrange("p (k t) -> p k t", k=2), dest_f[:]))
            v.tensor_copy(asg_i[:].rearrange("p (k t) -> p k t", k=2), asg_f[:]).then_inc(dest_ready, 1)

            def token_rows():
                link(v.tensor_copy(slot_f[:, 0, :], slot_i[:]))
                link(v.tensor_scalar(slot_f[:, 1, :], slot_f[:, 0, :], float(T), -float(T), ALU.is_ge, ALU.mult))
                link(v.tensor_tensor(slot_f[:, 1, :], slot_f[:, 0, :], slot_f[:, 1, :], ALU.add))
                return v.tensor_copy(tok_i[:], slot_f[:, 1, :])

            dve.wait_ge(slots_in, 16)
            token_rows().then_inc(slots_ready, 1)

            def copy_xT(e):
                dve.wait_ge(xg_transposed, e + 1)
                v.tensor_copy(xT[:, KT // 2:KT, :], PT[:, 1, :].rearrange("p (a b) -> p a b", a=KT // 2))\
                    .then_inc(xT_v, 1)

            def expert(c, i, b, last):
                e = c * E_ALL + i * 2 + b
                k = c * PAIRS + i
                dve.wait_ge(silu_done, e + 1)
                dve.wait_ge(hid_transposed, e)
                v.tensor_tensor(hid[0:CAP, :], silu[0:CAP, :], PJ[CAP:2 * CAP, 0:D_EXPERT], ALU.mult)\
                    .then_inc(hid_done, 1)
                if not (last and b == 1):
                    copy_xT(e + 1)
                dve.wait_ge(hid_transposed, e + 1)
                v.tensor_copy(hidT, Oflat[:, 0:2 * CAP].rearrange("p (a b) -> p a b", a=2)).then_inc(hidT_done, 1)
                dve.wait_ge(down_done, e + 1)
                dve.wait_ge(scattered[b], k * 16)
                v.tensor_copy(y_sb[b][0:CAP, D // 2:D].rearrange("p (m n) -> p m n", m=2), S[CAP:2 * CAP, 1, :, :])\
                    .then_inc(y_v, 1)

            def expert_pass(c):
                copy_xT(c * E_ALL)
                for b in range(2):
                    expert(c, 0, b, False)
                with dve.Fori(1, PAIRS - 1) as i:
                    for b in range(2):
                        expert(c, i, b, False)
                for b in range(2):
                    expert(c, PAIRS - 1, b, True)

            expert_pass(0)
            dve.wait_ge(most_ready, 1)
            most = dve.value_load(most_i[0:1, 0:1], min_val=0, max_val=T)
            with dve.If(most > CAP):
                with dve.Fori(1, PASSES) as c:
                    dve.wait_ge(pass_in, c * 16)
                    link.loop(c - 1, 3)
                    token_rows().then_inc(pass_ready, 1)
                    expert_pass(c)
                link.end(0)
            with dve.Else():
                dve.wait_ge(most_ready, 1)
            link = Chain(dve, end_chain)
            dve.wait_ge(lnf_in, 16)
            for step in range(NT + 1):
                if step < NT:
                    t = step
                    dve.wait_ge(y_in[t % 2], 32 * (t // 2 + 1))
                    xs = x_sb[:, t, :]
                    link(v.scalar_tensor_tensor(xs, y_rows[t % 2][0], wts[:, 0, t:t + 1], xs, ALU.mult, ALU.add))
                    v.scalar_tensor_tensor(xs, y_rows[t % 2][1], wts[:, 1, t:t + 1], xs, ALU.mult, ALU.add)\
                        .then_inc(y_added, 1)
                if step > 0:
                    t = step - 1
                    dve.wait_ge(f_sum, t + 1)
                    link(inverse_rms(t, NT + 3 + t))
                    if t >= 2:
                        dve.wait_ge(out_stored[t % 2], 16 * (t // 2))
                    v.scalar_tensor_tensor(out_sb[t % 2], x_sb[:, t, :], rstd[:, t:t + 1], lnf_sb, ALU.mult, ALU.mult)\
                        .then_inc(f_out, 1)


_INS = ["x", "ln1", "w_in", "diff_lambda", "diff_subln", "fox_bf", "cmp_pos_k", "cmp_w1_k", "cmp_w2_k",
        "cmp_pos_v", "cmp_w1_v", "cmp_w2_v", "t5_table", "w_out", "ln2", "router_group_w",
        "router_group_b", "router_expert_w", "router_expert_b", "w_gate", "w_up", "w_down", "ln_f"]


def kernel(**inputs):
    import concourse.bacc as bacc
    from concourse.bass_utils import run_bass_kernel_spmd as run

    nc = bacc.Bacc("TRN2", target_bir_lowering=False, num_devices=1)
    arrays, args = {}, []
    for name in _INS:
        a = np.ascontiguousarray(inputs[name])
        arrays[f"in_{name}"] = a
        args.append(nc.dram_tensor(f"in_{name}", a.shape, mybir.dt.from_np(a.dtype), kind="ExternalInput").ap())
    arrays["table"] = constants()
    args.append(nc.dram_tensor("table", (P, C_ALL), F32, kind="ExternalInput").ap())
    out = nc.dram_tensor("out", (1, T, D), F32, kind="ExternalOutput").ap()
    hybrid_block_moe_kernel(nc, *args, out)
    r = run(nc, [arrays], core_ids=[0])
    return r.results[0]["out"]
```
